# Optimizing a Trainium2 kernel written in Bass

```python
import jax, jax.numpy as jnp
from jax import lax
import numpy as np

D_MODEL = 1024
BATCH = 1
SEQ = 512
DEPTH = 2
DEC_BATCH = 1
DEC_SEQ = 64
PAST_LEN = 512

CHUNK = 64
Q_BLOCK = 128
HEAD_DIM = 64
N_HEADS = (3 * D_MODEL // 4) // HEAD_DIM
MIX_WIDTH = N_HEADS * HEAD_DIM
MEM_WIDTH = D_MODEL // 4
N_MEM_HEADS = MEM_WIDTH // HEAD_DIM
N_MEM = 256
D_FF = -(-8 * D_MODEL // (3 * 256)) * 256
N_FOX = (DEPTH + 1) // 2
N_SB = DEPTH // 2
FOX_IN = 3 * MIX_WIDTH + N_HEADS + MEM_WIDTH
SB_IN = 3 * MIX_WIDTH + MEM_WIDTH
EPS = 1e-6
SCALE = HEAD_DIM ** -0.5

kernel_name = "fox_stickbreak_memory_streaming_step"

def rmsnorm(x, g):
    xf = x.astype(jnp.float32)
    y = xf * lax.rsqrt(jnp.mean(xf * xf, axis=-1, keepdims=True) + EPS)
    return (y * g.astype(jnp.float32)).astype(x.dtype)

def to_blocks(a):
    b, t = a.shape[:2]
    return jnp.moveaxis(a.reshape((b, t // Q_BLOCK, Q_BLOCK) + a.shape[2:]), 1, 0)

def from_blocks(a):
    a = jnp.moveaxis(a, 0, 1)
    return a.reshape((a.shape[0], a.shape[1] * a.shape[2]) + a.shape[3:])

def fox_block(q, k, v, cq, ck, qpos, kpos):
    s = jnp.einsum('bqhd,bkhd->bhqk', q.astype(jnp.float32), k.astype(jnp.float32)) * SCALE
    s = s + jnp.transpose(cq, (0, 2, 1))[..., :, None] - jnp.transpose(ck, (0, 2, 1))[..., None, :]
    mask = kpos[None, :] <= qpos[:, None]
    p = jax.nn.softmax(jnp.where(mask, s, -jnp.inf), axis=-1)
    return jnp.einsum('bhqk,bkhd->bqhd', p.astype(v.dtype), v)

def sb_block(q, k, v, qpos, kpos):
    z = jnp.einsum('bqhd,bkhd->bhqk', q.astype(jnp.float32), k.astype(jnp.float32)) * SCALE
    mask = kpos[None, :] < qpos[:, None]
    u = jnp.where(mask, jax.nn.log_sigmoid(-z), 0.0)
    rest = lax.cumsum(u, axis=3, reverse=True) - u
    a = jnp.where(mask, jnp.exp(jax.nn.log_sigmoid(z) + rest), 0.0)
    return jnp.einsum('bhqk,bkhd->bqhd', a.astype(v.dtype), v)

def mem_attend(qm, mk, mv):
    s = jnp.einsum('bqhd,bmhd->bhqm', qm.astype(jnp.float32), mk.astype(jnp.float32)) * SCALE
    p = jax.nn.softmax(s, axis=-1)
    return jnp.einsum('bhqm,bmhd->bqhd', p.astype(mv.dtype), mv)

def heads(a, n):
    b, t = a.shape[:2]
    return a.reshape(b, t, n, HEAD_DIM)

def fox_mixer(hn, w_in, b_f, past):
    proj = hn @ w_in
    q, k, v, fg, qm = jnp.split(proj, [MIX_WIDTH, 2 * MIX_WIDTH, 3 * MIX_WIDTH, 3 * MIX_WIDTH + N_HEADS], axis=-1)
    q, k, v = heads(q, N_HEADS), heads(k, N_HEADS), heads(v, N_HEADS)
    logf = jax.nn.log_sigmoid((fg + b_f).astype(jnp.float32))
    t = hn.shape[1]
    if past is None:
        c = jnp.cumsum(logf, axis=1)
        pos = jnp.arange(t)
        def body(a):
            qb, cb, pb = a
            return fox_block(qb, k, v, cb, c, pb, pos)
        o = from_blocks(lax.map(body, (to_blocks(q), to_blocks(c), pos.reshape(-1, Q_BLOCK))))
    else:
        pk, pv, plf = past
        p_len = pk.shape[1]
        k_all = jnp.concatenate([pk.astype(k.dtype), k], axis=1)
        v_all = jnp.concatenate([pv.astype(v.dtype), v], axis=1)
        c_all = jnp.cumsum(jnp.concatenate([plf.astype(jnp.float32), logf], axis=1), axis=1)
        o = fox_block(q, k_all, v_all, c_all[:, p_len:], c_all, p_len + jnp.arange(t), jnp.arange(p_len + t))
    return o, heads(qm, N_MEM_HEADS), (k, v, logf)

def sb_mixer(hn, w_in, past):
    proj = hn @ w_in
    q, k, v, qm = jnp.split(proj, [MIX_WIDTH, 2 * MIX_WIDTH, 3 * MIX_WIDTH], axis=-1)
    q, k, v = heads(q, N_HEADS), heads(k, N_HEADS), heads(v, N_HEADS)
    t = hn.shape[1]
    if past is None:
        pos = jnp.arange(t)
        def body(a):
            qb, pb = a
            return sb_block(qb, k, v, pb, pos)
        o = from_blocks(lax.map(body, (to_blocks(q), pos.reshape(-1, Q_BLOCK))))
    else:
        pk, pv = past
        p_len = pk.shape[1]
        k_all = jnp.concatenate([pk.astype(k.dtype), k], axis=1)
        v_all = jnp.concatenate([pv.astype(v.dtype), v], axis=1)
        o = sb_block(q, k_all, v_all, p_len + jnp.arange(t), jnp.arange(p_len + t))
    return o, heads(qm, N_MEM_HEADS), (k, v)

def finish_layer(x, o_mix, qm, mk, mv, w_out, g_ffn, w_gate_up, w_down):
    b, t = x.shape[:2]
    o_mem = mem_attend(qm, mk, mv)
    o = jnp.concatenate([o_mix.reshape(b, t, MIX_WIDTH), o_mem.reshape(b, t, MEM_WIDTH)], axis=-1)
    x = x + o @ w_out
    gate, up = jnp.split(rmsnorm(x, g_ffn) @ w_gate_up, 2, axis=-1)
    return x + (jax.nn.silu(gate) * up) @ w_down

def setup_inputs(seed: int = 0) -> dict:
    key = jax.random.key(seed)
    ks = jax.random.split(key, 24)
    nrm = lambda k, shape, s=1.0: jax.random.normal(k, shape, jnp.float32) * s
    return {
        "x_prompt": nrm(ks[0], (BATCH, SEQ, D_MODEL)),
        "x_sample": nrm(ks[1], (DEC_BATCH, DEC_SEQ, D_MODEL)),
        "mem_prompt": nrm(ks[2], (BATCH, N_MEM, D_MODEL)),
        "cache_fox_k": nrm(ks[3], (N_FOX, DEC_BATCH, PAST_LEN, N_HEADS, HEAD_DIM)),
        "cache_fox_v": nrm(ks[4], (N_FOX, DEC_BATCH, PAST_LEN, N_HEADS, HEAD_DIM)),
        "cache_fox_logf": jax.nn.log_sigmoid(2.0 + nrm(ks[5], (N_FOX, DEC_BATCH, PAST_LEN, N_HEADS))),
        "cache_sb_k": nrm(ks[6], (N_SB, DEC_BATCH, PAST_LEN, N_HEADS, HEAD_DIM)),
        "cache_sb_v": nrm(ks[7], (N_SB, DEC_BATCH, PAST_LEN, N_HEADS, HEAD_DIM)),
        "cache_mem_k": nrm(ks[8], (DEPTH, DEC_BATCH, N_MEM, N_MEM_HEADS, HEAD_DIM)),
        "cache_mem_v": nrm(ks[9], (DEPTH, DEC_BATCH, N_MEM, N_MEM_HEADS, HEAD_DIM)),
        "g_mix": 1.0 + nrm(ks[10], (DEPTH, D_MODEL), 0.02),
        "w_in_fox": nrm(ks[11], (N_FOX, D_MODEL, FOX_IN), D_MODEL ** -0.5),
        "b_f": 2.0 + nrm(ks[12], (N_FOX, N_HEADS), 0.5),
        "w_in_sb": nrm(ks[13], (N_SB, D_MODEL, SB_IN), D_MODEL ** -0.5),
        "g_mem": 1.0 + nrm(ks[14], (DEPTH, D_MODEL), 0.02),
        "w_mem_kv": nrm(ks[15], (DEPTH, D_MODEL, 2 * MEM_WIDTH), D_MODEL ** -0.5),
        "w_out": nrm(ks[16], (DEPTH, MIX_WIDTH + MEM_WIDTH, D_MODEL), (MIX_WIDTH + MEM_WIDTH) ** -0.5),
        "g_ffn": 1.0 + nrm(ks[17], (DEPTH, D_MODEL), 0.02),
        "w_gate_up": nrm(ks[18], (DEPTH, D_MODEL, 2 * D_FF), D_MODEL ** -0.5),
        "w_down": nrm(ks[19], (DEPTH, D_FF, D_MODEL), D_FF ** -0.5),
        "g_final": 1.0 + nrm(ks[20], (D_MODEL,), 0.02),
    }

def reference(x_prompt, x_sample, mem_prompt, cache_fox_k, cache_fox_v, cache_fox_logf, cache_sb_k, cache_sb_v,
              cache_mem_k, cache_mem_v, g_mix, w_in_fox, b_f, w_in_sb, g_mem, w_mem_kv, w_out, g_ffn,
              w_gate_up, w_down, g_final):
    xp, xs = x_prompt, x_sample
    fk_p, fv_p, fl_p, sk_p, sv_p, mk_p_l, mv_p_l = [], [], [], [], [], [], []
    fk_s, fv_s, fl_s, sk_s, sv_s = [], [], [], [], []
    for i in range(DEPTH):
        j = i // 2
        mkv = rmsnorm(mem_prompt, g_mem[i]) @ w_mem_kv[i]
        mk_p, mv_p = jnp.split(mkv, 2, axis=-1)
        mk_p, mv_p = heads(mk_p, N_MEM_HEADS), heads(mv_p, N_MEM_HEADS)
        mk_p_l.append(mk_p)
        mv_p_l.append(mv_p)
        hp = rmsnorm(xp, g_mix[i])
        hs = rmsnorm(xs, g_mix[i])
        if i % 2 == 0:
            op, qmp, (k, v, lf) = fox_mixer(hp, w_in_fox[j], b_f[j], None)
            os_, qms, (k2, v2, lf2) = fox_mixer(hs, w_in_fox[j], b_f[j],
                                                (cache_fox_k[j], cache_fox_v[j], cache_fox_logf[j]))
            fk_p.append(k); fv_p.append(v); fl_p.append(lf)
            fk_s.append(k2); fv_s.append(v2); fl_s.append(lf2)
        else:
            op, qmp, (k, v) = sb_mixer(hp, w_in_sb[j], None)
            os_, qms, (k2, v2) = sb_mixer(hs, w_in_sb[j], (cache_sb_k[j], cache_sb_v[j]))
            sk_p.append(k); sv_p.append(v)
            sk_s.append(k2); sv_s.append(v2)
        xp = finish_layer(xp, op, qmp, mk_p, mv_p, w_out[i], g_ffn[i], w_gate_up[i], w_down[i])
        xs = finish_layer(xs, os_, qms, cache_mem_k[i].astype(xs.dtype), cache_mem_v[i].astype(xs.dtype),
                          w_out[i], g_ffn[i], w_gate_up[i], w_down[i])
    y_prompt = rmsnorm(xp, g_final)
    y_sample = rmsnorm(xs, g_final)
    return (y_prompt, y_sample,
            jnp.stack(fk_p), jnp.stack(fv_p), jnp.stack(fl_p), jnp.stack(sk_p), jnp.stack(sv_p),
            jnp.stack(mk_p_l), jnp.stack(mv_p_l),
            jnp.stack(fk_s), jnp.stack(fv_s), jnp.stack(fl_s), jnp.stack(sk_s), jnp.stack(sv_s))


_drawn_inputs = setup_inputs


def setup_inputs(seed=0):
    import zlib

    import numpy as np

    out = dict(_drawn_inputs(seed))
    spreads = {}
    factors = {'g_mem': 2.76, 'g_ffn': 2.871, 'g_final': 8.632, 'cache_sb_k': 8.0, 'cache_sb_v': 3.172}
    for name, (base, spread) in spreads.items():
        noise = np.random.default_rng([zlib.crc32(name.encode()), seed]).standard_normal(out[name].shape)
        drawn = base * np.exp(spread * noise) if base else spread * noise
        out[name] = __import__('jax').numpy.asarray(drawn.astype(out[name].dtype))
    for name, factor in factors.items():
        out[name] = (out[name] * factor).astype(out[name].dtype)
    return out
```

```python
from contextlib import ExitStack

import concourse.bass as bass
import concourse.mybir as mybir
import numpy as np
from concourse.alu_op_type import AluOpType as ALU

F32 = mybir.dt.float32
F32R = mybir.dt.float32r
ACT = mybir.ActivationFunctionType
AX = mybir.AxisListType.X

P = 128
D_MODEL = 1024
SEQ = 512
DEC = 64
PAST = 512
DEPTH = 2
HD = 64
HEADS = 12
N_MEM = 256
MEM_HEADS = 4
D_FF = 2816
EPS = 1e-6
SCALE = HD ** -0.5
BIG = 1e30

TOK = DEC + SEQ
HALF = TOK // 2
KT = D_MODEL // P
FT = D_FF // P
PAIRS = HEADS // 2
MEM_PAIRS = MEM_HEADS // 2
QT = SEQ // P
MB = N_MEM // P
KEYS_S = PAST + DEC
SLAB = KT * P
IN_TILES = 2 + 3 * PAIRS
OUT_TILES = KT
GU_TILES = 2 * FT
DOWN_CUTS = (8, 8, 6)
MKV_TILES = 4

MKV_SLABS = DEPTH * MKV_TILES
LAYER_TILES = IN_TILES + OUT_TILES + GU_TILES + KT
LAYER_SLABS = IN_TILES + OUT_TILES + GU_TILES + 3 * KT
ATTNS = MEM_PAIRS + PAIRS
UNITS = 2 * QT + 1
USES = 2 * QT + 2

C_ID, C_ONES, C_FOX, C_FOXS, C_SBN, C_SBNS, C_SB1, C_SB1S = 0, 128, 256, 384, 448, 576, 640, 768
C_END = 832


def at_least(eng, sem, value):
    if not (isinstance(value, int) and value <= 0):
        eng.wait_ge(sem, value)


def build(nc, x_t, mem_t, w_mkv, w_in, w_f, w_out, w_gu, w_dn, gains, b_f, ck, cv, clf, cmk, cmv,
          consts, y_t, k_o, v_o, lf_o, mk_o, mv_o):
    ctx = ExitStack()
    region = ExitStack()

    def sb(name, shape, dt=F32, stack=ctx):
        return stack.enter_context(nc.sbuf_tensor(name, shape, dt))

    x = sb("x", [P, KT, TOK])
    xg_hi = sb("xg_hi", [P, KT, TOK], F32R)
    xg_lo = sb("xg_lo", [P, KT, TOK], F32R)
    w_raw = sb("w_raw", [P, 2, SLAB])
    w_hi = [sb(f"w_hi{i}", [P, SLAB], F32R) for i in range(2)]
    w_lo = [sb(f"w_lo{i}", [P, SLAB], F32R) for i in range(2)]
    cst = sb("cst", [P, C_END])
    gain = sb("gain", [P, 7 * KT])
    mk = sb("mk", [P, DEPTH, MEM_PAIRS, N_MEM])
    mv = sb("mv", [P, DEPTH, MEM_PAIRS, MB * P])
    rstd = sb("rstd", [P, TOK])
    sumsq = sb("sumsq", [P, TOK])
    work_a = sb("work_a", [P, 2, TOK])
    work_b = sb("work_b", [P, 2, TOK])
    work_c = sb("work_c", [P, 2, TOK])
    least = sb("least", [P, 2])
    total = sb("total", [P, 2])
    inv = sb("inv", [P, 2])
    cq = sb("cq", [P, QT, HEADS])
    cq_s = sb("cq_s", [P, PAIRS])

    at = lambda name, shape, dt=F32: sb(name, shape, dt, region)
    qz = [at(f"qz{i}", [P, 2, TOK]) for i in range(2)]
    qs = [at(f"qs{i}", [P, 2 * DEC]) for i in range(2)]
    kb = [at(f"kb{i}", [P, PAST + TOK]) for i in range(2)]
    vc = [at(f"vc{i}", [P, QT, P]) for i in range(2)]
    v = [at(f"v{i}", [P, QT, P]) for i in range(2)]
    vn = [at(f"vn{i}", [P, P]) for i in range(2)]
    vf_z = at("vf_z", [P, DEC + TOK])
    vf = vf_z[:, DEC:]
    pt = at("pt", [P, QT, SEQ])
    pts = at("pts", [P, QT * P + P])
    ckb = [at(f"ckb{i}", [P, 2, SEQ]) for i in range(2)]
    ckbs = [at(f"ckbs{i}", [P, KEYS_S]) for i in range(2)]
    cum = at("cum", [HEADS, PAST + TOK])
    wf_raw = at("wf_raw", [P, KT * HEADS])
    wf_hi = at("wf_hi", [P, KT * HEADS], F32R)
    wf_lo = at("wf_lo", [P, KT * HEADS], F32R)
    bias_f = at("bias_f", [HEADS, 1])
    dup = sb("dup", [HEADS, P], F32, region)
    lf = sb("lf", [HEADS, PAST + TOK], F32, region)
    inner = ExitStack()
    o_hi = sb("o_hi", [P, KT, TOK], F32R, inner)
    o_lo = sb("o_lo", [P, KT, TOK], F32R, inner)
    inner.close()
    m_raw = sb("m_raw", [P, KT, N_MEM], F32, region)
    m_hi = sb("m_hi", [P, KT, N_MEM], F32R, region)
    m_lo = sb("m_lo", [P, KT, N_MEM], F32R, region)
    m_sq = sb("m_sq", [P, KT, N_MEM], F32, region)
    region.close()
    f_hi = sb("f_hi", [P, FT, TOK], F32R)
    f_lo = sb("f_lo", [P, FT, TOK], F32R)
    rstd_m = rstd[:, 0:N_MEM]
    mvt = pt[:, :, 0:N_MEM]

    psum = lambda name, shape: ctx.enter_context(nc.psum_tensor(name, shape, F32))
    acc = psum("acc", [P, 2, 2, 512])
    score = psum("score", [P, 2, 512])
    turned = psum("turned", [P, 512])
    out_ps = psum("out_ps", [P, 512])

    sem = lambda name: ctx.enter_context(nc.semaphore(name))
    const_in = sem("const_in")
    x_in = sem("x_in")
    mem_in = sem("mem_in")
    w_arrived = [sem(f"w_arrived{i}") for i in range(2)]
    whi_made = sem("whi_made")
    wlo_made = sem("wlo_made")
    slab_done = sem("slab_done")
    acc_free = sem("acc_free")
    score_ready = sem("score_ready")
    score_free = sem("score_free")
    exp_in = sem("exp_in")
    exp_out = sem("exp_out")
    probs_ready = sem("probs_ready")
    soft_ready = sem("soft_ready")
    turned_ready = sem("turned_ready")
    turned_free = sem("turned_free")
    out_ready = sem("out_ready")
    out_hi = sem("out_hi")
    out_free = sem("out_free")
    qkv_ready = sem("qkv_ready")
    cache_in = [sem(f"cache_in{i}") for i in range(2)]
    cum_in = [sem(f"cum_in{i}") for i in range(2)]
    kv_stored = sem("kv_stored")
    mem_stored = sem("mem_stored")
    x_new = sem("x_new")
    xhi_made = sem("xhi_made")
    xlo_made = sem("xlo_made")
    sq_made = sem("sq_made")
    sq_added = sem("sq_added")
    mean_ready = sem("mean_ready")
    root_ready = sem("root_ready")
    m_hi_made = sem("m_hi_made")
    m_lo_made = sem("m_lo_made")
    m_sq_made = sem("m_sq_made")
    mem_kv = sem("mem_kv")
    wf_in = sem("wf_in")
    wf_hi_made = sem("wf_hi_made")
    wf_lo_made = sem("wf_lo_made")
    zeroed = sem("zeroed")
    gate_in = sem("gate_in")
    gate_soft = sem("gate_soft")
    lf_made = sem("lf_made")
    cum_made = sem("cum_made")
    clf_in = sem("clf_in")
    lf_stored = sem("lf_stored")
    cum_out = sem("cum_out")
    gated = sem("gated")
    silu_made = sem("silu_made")
    prod_made = sem("prod_made")
    fhi_made = sem("fhi_made")
    flo_made = sem("flo_made")
    y_made = sem("y_made")
    y_stored = sem("y_stored")
    cum_dram = nc.dram_tensor("cum_dram", (HEADS, PAST + TOK), F32).ap()

    ident = cst[:, C_ID:C_ID + P]
    ones = cst[:, C_ONES:C_ONES + P]

    def halves(tile):
        return tile.rearrange("p (h c) -> p h c", h=2)

    def layer_slab(layer):
        return MKV_SLABS + layer * LAYER_SLABS

    def gu_slab(layer):
        return layer_slab(layer) + IN_TILES + OUT_TILES

    def layer_tile(layer):
        return MKV_SLABS + layer * LAYER_TILES

    LAYER_USE = [2, 8 + ATTNS * USES, 12 + 2 * ATTNS * USES]

    def attn_use(layer, a):
        return LAYER_USE[layer] + (4 if layer == 0 else 2) + a * USES

    MEM_ROUNDS = 2 * QT + 1
    PAIR_ROUNDS = 2 + 2 * QT + 2
    LAYER_ROUNDS = MEM_PAIRS * MEM_ROUNDS + PAIRS * PAIR_ROUNDS

    class Call:

        def __init__(self, layer, half, par, fill, mem):
            self.layer, self.half, self.par, self.fill, self.mem = layer, half, par, fill, mem
            self.a = a = half * 2 + par
            self.pair = None if mem else a - MEM_PAIRS
            self.o_tile = PAIRS + a if mem else a - MEM_PAIRS
            self.unit = (a + layer * ATTNS) * UNITS
            self.use = attn_use(layer, a)
            first = 2 * DEPTH + 1 + layer * LAYER_ROUNDS
            self.round = a * MEM_ROUNDS + first if mem else \
                a * PAIR_ROUNDS + (first + MEM_PAIRS * (MEM_ROUNDS - PAIR_ROUNDS))
            self.unit_round = self.round if mem else self.round + 2
            self.end_round = self.round + (MEM_ROUNDS if mem else PAIR_ROUNDS)
            self.out = (a + layer * ATTNS) * 3
            self.qkv = layer * IN_TILES + a + 1 if mem else a * 3 + (layer * IN_TILES - 1)
            self.caches = (half + (layer * ATTNS // 2 + 1)) * 32
            self.cums = half * 64
            self.fpar = 1 - par
            if fill is not None:
                self.fill_slab = fill * 6 + (layer_slab(layer) + 2 + 3 * self.fpar)
                self.fill_tile = fill * 6 + (layer_tile(layer) + 2 + 3 * self.fpar)

        def buf(self, u):
            return (self.par + u) % 2

        def width(self, u):
            if u == 2 * QT:
                return N_MEM if self.mem else KEYS_S
            return N_MEM if self.mem else (u % QT + 1) * P

    def calls(eng, layer, call):
        call(Call(layer, 0, 0, None, True))
        call(Call(layer, 0, 1, 0, True))
        with eng.Fori(0, (PAIRS - 2) // 2) as i:
            call(Call(layer, i + 1, 0, i, False))
            call(Call(layer, i + 1, 1, i + 1, False))
        call(Call(layer, ATTNS // 2 - 1, 0, PAIRS // 2 - 1, False))
        call(Call(layer, ATTNS // 2 - 1, 1, None, False))

    block = ctx.enter_context(nc.Block())

    @block.sync
    def _(sp):
        sp.dma_start(m_raw[:, :, :], mem_t).then_inc(mem_in, 16)
        sp.dma_start(gain[:, :], gains).then_inc(const_in, 16)
        sp.dma_start(cst[:, :], consts).then_inc(const_in, 16)

        def slab(s, par, src, cols=SLAB):
            at_least(sp, wlo_made, s - 1)
            sp.dma_start(w_raw[:, par, 0:cols], src).then_inc(w_arrived[par], 16)

        def cache(layer, half, par, mem):
            c = Call(layer, half, par, None, mem)
            at_least(sp, out_ready, 0 if layer == 0 and mem else c.out - 3)
            if mem:
                sp.dma_start(kb[par][:, 0:N_MEM], cmk[layer, par]).then_inc(cache_in[par], 16)
                sp.dma_start(vc[par][:, 0:MB, :], cmv[layer, par].rearrange("p (j c) -> p j c", j=MB)) \
                    .then_inc(cache_in[par], 16)
                return
            sp.dma_start(kb[par][:, 0:PAST], ck[layer, bass.ds(c.pair, 1)].rearrange("a p c -> (a p) c")) \
                .then_inc(cache_in[par], 16)
            sp.dma_start(vc[par][:, :, :], cv[layer, bass.ds(c.pair, 1)].rearrange("a p (j c) -> (a p) j c", j=QT)) \
                .then_inc(cache_in[par], 16)
            if layer == 0:
                sp.wait_ge(cum_out, 16)
                for hd in range(2):
                    row = cum_dram[bass.ds(c.pair * 2 + hd, 1), :]
                    sp.dma_start(ckb[par][:, hd, :], row[:, KEYS_S:].to_broadcast([P, SEQ])) \
                        .then_inc(cum_in[par], 16)
                    sp.dma_start(ckbs[par][hd * HD:(hd + 1) * HD, :],
                                 row[:, 0:KEYS_S].to_broadcast([HD, KEYS_S])).then_inc(cum_in[par], 16)

        for s in range(2):
            slab(s, s, w_mkv[0, s])
        sp.dma_start(x[:, :, :], x_t).then_inc(x_in, 16)
        sp.dma_start(wf_raw[:, :], w_f).then_inc(wf_in, 16)
        sp.dma_start(bias_f[:, :], b_f).then_inc(wf_in, 16)
        sp.dma_start(lf[:, 0:PAST], clf).then_inc(clf_in, 16)
        for s in range(2, MKV_SLABS):
            slab(s, s % 2, w_mkv[s // MKV_TILES, s % MKV_TILES])
        for layer in range(DEPTH):
            s0 = layer_slab(layer)
            for t in range(2):
                slab(s0 + t, t, w_in[layer, t])
            if layer:
                sp.wait_ge(slab_done, s0)
            cache(layer, 0, 0, True)
            cache(layer, 0, 1, True)
            with sp.Fori(0, PAIRS // 2) as i:
                for par in range(2):
                    for c in range(3):
                        t = 2 + 3 * par + c
                        slab(i * 6 + (s0 + t), t % 2,
                             w_in[layer, bass.ds(i * 6 + t, 1)].rearrange("a p c -> (a p) c"))
                        if c == 1:
                            cache(layer, i + 1, par, False)
            for first, src, count in ((s0 + IN_TILES, w_out, OUT_TILES), (gu_slab(layer), w_gu, GU_TILES)):
                with sp.Fori(0, count // 2) as i:
                    for j in range(2):
                        slab(i * 2 + (first + j), j,
                             src[layer, bass.ds(i * 2 + j, 1)].rearrange("a p c -> (a p) c"))
            with sp.Fori(0, KT // 2) as i:
                for n in range(6):
                    m, c = divmod(n, 3)
                    cols = DOWN_CUTS[c] * P
                    src = w_dn[layer, bass.ds(i * 2 + m, 1)].rearrange("a p c -> (a p) c")
                    slab(i * 6 + (gu_slab(layer) + GU_TILES + n), n % 2,
                         src[:, c * SLAB:c * SLAB + cols], cols)
        for k in range(KT):
            sp.wait_ge(y_made, k + 1)
            sp.dma_start(y_t[:, k, :], x[:, k, :]).then_inc(y_stored, 16)
        sp.wait_ge(y_stored, 16 * KT)
        sp.wait_ge(kv_stored, 32 * DEPTH * PAIRS)
        sp.wait_ge(mem_stored, 16 * MKV_SLABS)
        sp.wait_ge(lf_stored, 16)

    @block.gpsimd
    def _(pool):
        def low(s, par, cols=SLAB):
            pool.wait_ge(whi_made, s + 1)
            pool.tensor_tensor(w_lo[par][:, 0:cols], w_raw[:, par, 0:cols],
                               w_hi[par][:, 0:cols].bitcast(F32), ALU.subtract).then_inc(wlo_made, 1)

        def add_square(norm, m):
            if m:
                if m > 1:
                    pool.wait_ge(sq_added, norm * (KT - 1) + m - 1)
                pool.wait_ge(sq_made, norm * KT + m + 1)
                pool.tensor_tensor(sumsq[:, :], sumsq[:, :], work_c[:, m % 2, :], ALU.add) \
                    .then_inc(sq_added, 1)

        def zero_rows(layer):
            tiles = [vf_z[:, 0:DEC]]
            for par in range(2):
                tiles += [qz[par][HD:P, 0, :], qz[par][0:HD, 1, :], qs[par][HD:P, 0:DEC], qs[par][0:HD, DEC:]]
            for n, tile in enumerate(tiles):
                pool.memset(tile, 0.0).then_inc(zeroed, 1)
                pool.wait_ge(zeroed, len(tiles) * layer + n + 1)

        for s in range(MKV_SLABS):
            low(s, s % 2)
            add_square(0, s)
        pool.wait_ge(wf_hi_made, 1)
        pool.tensor_tensor(wf_lo[:, :], wf_raw[:, :], wf_hi[:, :].bitcast(F32), ALU.subtract) \
            .then_inc(wf_lo_made, 1)
        for layer in range(DEPTH):
            s0 = layer_slab(layer)
            low(s0, 0)
            low(s0 + 1, 1)
            if layer:
                pool.wait_ge(slab_done, s0)
            zero_rows(layer)
            with pool.Fori(1, IN_TILES // 2) as i:
                for j in range(2):
                    low(i * 2 + (s0 + j), j)
            for m in range(OUT_TILES):
                low(s0 + IN_TILES + m, m % 2)
                if m:
                    add_square(2 * layer + 1, m - 1)
            low(gu_slab(layer), 0)
            add_square(2 * layer + 1, KT - 1)
            low(gu_slab(layer) + 1, 1)
            with pool.Fori(1, GU_TILES // 2) as i:
                for j in range(2):
                    low(i * 2 + (gu_slab(layer) + j), j)
            for m in range(KT):
                for c, cut in enumerate(DOWN_CUTS):
                    low(gu_slab(layer) + GU_TILES + 3 * m + c, (3 * m + c) % 2, cut * P)
                if m:
                    add_square(2 * layer + 2, m - 1)
            add_square(2 * layer + 2, KT - 1)

    @block.tensor
    def _(pe):
        def passes(par, k, hi, lo, tpar, first, last):
            width = hi.shape[-1]
            cuts = ((0, HALF), (HALF, TOK)) if width == TOK else ((0, width),)
            parts = ((w_hi, hi), (w_hi, lo), (w_lo, hi))
            for n, (w, a) in enumerate(parts):
                for h, (c0, c1) in enumerate(cuts):
                    mm = pe.matmul(acc[:, tpar, h, 0:c1 - c0], w[par][:, k * P:(k + 1) * P], a[:, c0:c1],
                                   start=first and n == 0, stop=last and n == 2)
            return mm

        def begin(s, t):
            pe.wait_ge(wlo_made, s + 1)
            at_least(pe, acc_free, t - 1)

        def product(s, t, par, tpar, hi, lo, kts=KT, k0=0, first=True, last=True, before=None):
            begin(s, t)
            for k in range(kts):
                if before is not None:
                    before(k0 + k)
                mm = passes(par, k, hi[:, k0 + k, :], lo[:, k0 + k, :], tpar,
                            first and k == 0, last and k == kts - 1)
            mm.then_inc(slab_done, 1)

        def norm_sum(norm, use):
            pe.wait_ge(sq_added, (KT - 1) * (norm + 1))
            pe.wait_ge(score_free, use)
            for h in range(2):
                pe.matmul(score[:, h, 0:HALF], ones, sumsq[:, h * HALF:(h + 1) * HALF],
                          start=True, stop=True).then_inc(score_ready, 1)

        pe.wait_ge(const_in, 32)
        pe.wait_ge(m_sq_made, 1)
        for h in range(2):
            for k in range(KT):
                mm = pe.matmul(score[:, h, 0:P], ones, m_sq[:, k, h * P:(h + 1) * P],
                               start=(k == 0), stop=(k == KT - 1))
            mm.then_inc(score_ready, 1)

        def turn_mem(s):
            n = 2 * (s // MKV_TILES) + s % 2
            pe.wait_ge(mem_kv, s + 1)
            at_least(pe, turned_free, n)
            for j in range(MB):
                mm = pe.transpose(turned[:, j * P:(j + 1) * P], mvt[:, n, j * P:(j + 1) * P], ident)
            mm.then_inc(turned_ready, 1)

        for s in range(MKV_SLABS):
            pe.wait_ge(m_lo_made, KT * (s // MKV_TILES + 1))
            product(s, s, s % 2, s % 2, m_hi, m_lo)
            if s and (s - 1) % MKV_TILES >= 2:
                turn_mem(s - 1)
        turn_mem(MKV_SLABS - 1)

        spread = [KT * 3 * u // UNITS for u in range(UNITS + 1)]

        def attention(c):
            layer, par, mem = c.layer, c.par, c.mem

            def fill_part(u):
                if c.fill is None:
                    return
                for g in range(spread[u], spread[u + 1]):
                    n, k = divmod(g, KT)
                    slot = (c.fpar + n) % 2
                    if k == 0:
                        begin(c.fill_slab + n, c.fill_tile + n)
                    mm = passes(slot, k, xg_hi[:, k, :], xg_lo[:, k, :], slot, k == 0, k == KT - 1)
                    if k == KT - 1:
                        mm.then_inc(slab_done, 1)

            def scores(u):
                if u == 2 * QT:
                    width = c.width(u) // 2
                    pe.wait_ge(cache_in[par], c.caches)
                    pe.wait_ge(score_free, c.use + u)
                    for h in range(2):
                        pe.matmul(score[:, h, 0:width], qs[par][:, :],
                                  kb[par][:, h * width:(h + 1) * width],
                                  start=True, stop=True).then_inc(score_ready, 1)
                    return
                hd, i = divmod(u, QT)
                width = c.width(u)
                keys = mk[:, layer, par, :] if mem else kb[par][:, KEYS_S:KEYS_S + width]
                pe.wait_ge(score_free, c.use + (u - 1))
                pe.matmul(score[:, u % 2, 0:width], qz[par][:, hd, DEC + i * P:DEC + (i + 1) * P], keys,
                          start=True, stop=True).then_inc(score_ready, 1)

            def turn(u):
                probs = work_b[:, c.buf(u), :]
                pe.wait_ge(probs_ready, c.unit + (u + 1))
                pe.wait_ge(turned_free, c.unit_round + u)
                for j in range(c.width(u) // P):
                    mm = pe.transpose(turned[:, j * P:(j + 1) * P], probs[:, j * P:(j + 1) * P], ident)
                mm.then_inc(turned_ready, 1)
                if u == 2 * QT and not mem:
                    pe.wait_ge(turned_free, c.unit_round + (u + 1))
                    pe.transpose(turned[:, 0:P], probs[:, KEYS_S - P:KEYS_S], ident).then_inc(turned_ready, 1)

            def values(hd):
                pe.wait_ge(turned_free, c.unit_round + QT * (hd + 1))
                at_least(pe, out_free, c.out + hd)
                count = MB if mem else QT
                for j in range(count):
                    c0 = 0 if mem else j * P
                    val = mv[:, layer, par, j * P:(j + 1) * P] if mem else v[par][:, j, :]
                    mm = pe.matmul(out_ps[:, c0:SEQ], val, pt[:, j, c0:SEQ], start=(j == 0),
                                   stop=(j == count - 1), skip_group_check=True)
                mm.then_inc(out_ready, 1)

            def values_sample():
                pe.wait_ge(turned_free, c.end_round)
                pe.wait_ge(out_free, c.out + 2)
                count = MB if mem else QT
                for j in range(count):
                    mm = pe.matmul(out_ps[:, 0:P], vc[par][:, j, :], pts[:, j * P:(j + 1) * P],
                                   start=(j == 0), stop=(mem and j == count - 1))
                if not mem:
                    mm = pe.matmul(out_ps[:, 0:P], vn[par][:, :], pts[:, QT * P:],
                                   start=False, stop=True)
                mm.then_inc(out_ready, 1)

            pe.wait_ge(qkv_ready, c.qkv)
            if not mem:
                pe.wait_ge(turned_free, c.round)
                for j in range(QT):
                    mm = pe.transpose(turned[:, j * P:(j + 1) * P],
                                      vf[:, DEC + j * P:DEC + (j + 1) * P], ident)
                mm.then_inc(turned_ready, 1)
            scores(0)
            scores(1)
            if not mem:
                pe.wait_ge(turned_free, c.round + 1)
                pe.transpose(turned[:, 0:P], vf_z[:, 0:P], ident).then_inc(turned_ready, 1)
            for u in range(UNITS):
                fill_part(u)
                if u == QT:
                    values(0)
                if u == 2 * QT:
                    values(1)
                turn(u)
                if u + 2 < UNITS:
                    scores(u + 2)
            values_sample()

        for layer in range(DEPTH):
            s0, t0 = layer_slab(layer), layer_tile(layer)
            product(s0, t0, 0, 0, xg_hi, xg_lo,
                    before=lambda k: pe.wait_ge(xlo_made, KT * 2 * layer + k + 1))
            norm_sum(2 * layer, LAYER_USE[layer])
            if layer == 0:
                pe.wait_ge(wf_lo_made, 1)
                pe.wait_ge(score_free, LAYER_USE[layer] + 2)
                for h in range(2):
                    for k in range(KT):
                        parts = ((wf_hi, xg_hi), (wf_hi, xg_lo), (wf_lo, xg_hi))
                        for n, (w, a) in enumerate(parts):
                            mm = pe.matmul(score[0:HEADS, h, 0:HALF], w[:, k * HEADS:(k + 1) * HEADS],
                                           a[:, k, h * HALF:(h + 1) * HALF],
                                           start=(k == 0 and n == 0), stop=(k == KT - 1 and n == 2))
                    mm.then_inc(score_ready, 1)
            product(s0 + 1, t0 + 1, 1, 1, xg_hi, xg_lo)
            if layer == 0:
                pe.wait_ge(cum_made, 1)
                pe.wait_ge(turned_free, 2 * DEPTH)
                for i in range(QT):
                    pe.transpose(turned[:, i * HEADS:(i + 1) * HEADS],
                                 cum[:, KEYS_S + i * P:KEYS_S + (i + 1) * P], ident[0:HEADS, 0:HEADS])
                pe.transpose(turned[:, QT * HEADS:(QT + 1) * HEADS], dup[:, :],
                             ident[0:HEADS, 0:HEADS]).then_inc(turned_ready, 1)
            pe.wait_ge(zeroed, 9 * (layer + 1))
            calls(pe, layer, attention)

            so, to = s0 + IN_TILES, t0 + IN_TILES
            pe.wait_ge(out_free, 3 * ATTNS * (layer + 1))
            with pe.Fori(0, OUT_TILES // 2) as i:
                for j in range(2):
                    product(i * 2 + (so + j), i * 2 + (to + j), j, j, o_hi, o_lo)

            sg, tg = so + OUT_TILES, to + OUT_TILES
            product(sg, tg, 0, 0, xg_hi, xg_lo,
                    before=lambda k: pe.wait_ge(xlo_made, KT * (2 * layer + 1) + k + 1))
            norm_sum(2 * layer + 1, attn_use(layer, ATTNS))
            product(sg + 1, tg + 1, 1, 1, xg_hi, xg_lo)
            with pe.Fori(1, GU_TILES // 2) as i:
                for j in range(2):
                    product(i * 2 + (sg + j), i * 2 + (tg + j), j, j, xg_hi, xg_lo)

            sd, td = sg + GU_TILES, tg + GU_TILES

            def down(i, m, before=None):
                k0 = 0
                for n, cut in enumerate(DOWN_CUTS):
                    product(i * 6 + (sd + 3 * m + n), i * 2 + (td + m), (3 * m + n) % 2, m, f_hi, f_lo, cut, k0,
                            n == 0, n == len(DOWN_CUTS) - 1, before)
                    k0 += cut

            down(0, 0, lambda k: pe.wait_ge(flo_made, layer * FT + k + 1))
            down(0, 1)
            with pe.Fori(1, KT // 2) as i:
                down(i, 0)
                down(i, 1)
        norm_sum(2 * DEPTH, LAYER_USE[DEPTH])

    @block.scalar
    def _(act):
        def high(s, par, cols=SLAB):
            act.wait_ge(w_arrived[par], (s - par) * 8 + 16)
            at_least(act, slab_done, s - 1)
            act.activation(w_hi[par][:, 0:cols], w_raw[:, par, 0:cols], ACT.Copy).then_inc(whi_made, 1)

        def root(norm):
            act.wait_ge(mean_ready, norm + 1)
            width = N_MEM if norm == 0 else TOK
            act.activation(rstd[:, 0:width], rstd[:, 0:width], ACT.Sqrt).then_inc(root_ready, 1)

        def split_x(norm, m, g):
            if norm:
                act.wait_ge(x_new, KT * (norm - 1) + m + 1)
            if g is not None:
                act.activation(xg_hi[:, m, :], x[:, m, :], ACT.Copy,
                               scale=gain[:, g * KT + m:g * KT + m + 1]).then_inc(xhi_made, 1)
            if m > 2:
                act.wait_ge(sq_added, (KT - 1) * norm + m - 2)
            square = sumsq[:, :] if m == 0 else work_c[:, m % 2, :]
            act.activation(square, x[:, m, :], ACT.Square).then_inc(sq_made, 1)

        high(0, 0)
        act.wait_ge(const_in, 32)
        act.wait_ge(mem_in, 16)
        act.activation(m_sq[:, :, :], m_raw[:, :, :], ACT.Square).then_inc(m_sq_made, 1)

        def split_mem(layer):
            for k in range(KT):
                c = (2 + layer) * KT + k
                act.activation(m_hi[:, k, :], m_raw[:, k, :], ACT.Copy, scale=gain[:, c:c + 1]) \
                    .then_inc(m_hi_made, 1)

        split_mem(0)
        high(1, 1)
        root(0)
        act.wait_ge(x_in, 16)

        def copy_mem(s):
            n = 2 * (s // MKV_TILES) + s % 2
            act.wait_ge(turned_ready, n + 1)
            act.activation(mv[:, s // MKV_TILES, s % 2, :], turned[:, 0:N_MEM], ACT.Copy) \
                .then_inc(turned_free, 1)

        for s in range(MKV_SLABS):
            if s == MKV_TILES:
                act.wait_ge(slab_done, s)
                split_mem(1)
            if s:
                high(s + 1, (s + 1) % 2)
            split_x(0, s, 0)
            layer, c = divmod(s, MKV_TILES)
            act.wait_ge(mem_kv, s + 1)
            source = mk[:, layer, c, :] if c < 2 else mvt[:, 2 * layer + c - 2, :]
            act.dma_start((mk_o if c < 2 else mv_o)[layer, c % 2], source).then_inc(mem_stored, 16)
            if s and (s - 1) % MKV_TILES >= 2:
                copy_mem(s - 1)
        copy_mem(MKV_SLABS - 1)
        act.wait_ge(wf_in, 32)
        act.activation(wf_hi[:, :], wf_raw[:, :], ACT.Copy).then_inc(wf_hi_made, 1)

        def attention(c):
            layer, par, mem = c.layer, c.par, c.mem
            stick = layer == 1 and not mem

            def softplus(u):
                b, w = c.buf(u), c.width(u)
                if u == 2 * QT:
                    act.wait_ge(score_ready, c.use + (u + 2))
                    z, out = score[:, :, 0:HALF], halves(work_c[:, b, :])
                else:
                    act.wait_ge(score_ready, c.use + (u + 1))
                    z, out = score[:, u % 2, 0:w], work_c[:, b, 0:w]
                act.activation(out, z, ACT.Abs)
                act.drain()
                flat = work_c[:, b, 0:w]
                act.activation(flat, flat, ACT.Exp, scale=-1.0)
                act.drain()
                act.activation(flat, flat, ACT.Ln, bias=1.0).then_inc(soft_ready, 1)

            def exponential(u):
                b, w = c.buf(u), c.width(u)
                act.wait_ge(exp_in, c.unit + (u + 1))
                if stick:
                    act.activation(work_b[:, b, 0:w], work_a[:, b, 0:w], ACT.Exp).then_inc(probs_ready, 1)
                else:
                    act.activation(work_b[:, b, 0:w], work_a[:, b, 0:w], ACT.Exp, bias=least[:, b:b + 1],
                                   scale=-1.0, accum_out=total[:, b:b + 1]).then_inc(exp_out, 1)

            def copy_turned(u):
                act.wait_ge(turned_ready, c.unit_round + (u + 1))
                n = c.width(u) // P
                if u < 2 * QT:
                    i = u % QT
                    act.activation(pt[:, 0:n, i * P:(i + 1) * P],
                                   turned[:, 0:n * P].rearrange("p (j q) -> p j q", j=n), ACT.Copy) \
                        .then_inc(turned_free, 1)
                    return
                act.activation(pts[:, 0:n * P], turned[:, 0:n * P], ACT.Copy).then_inc(turned_free, 1)
                if not mem:
                    act.wait_ge(turned_ready, c.end_round)
                    act.activation(pts[:, QT * P:], turned[:, 0:P], ACT.Copy) \
                        .then_inc(turned_free, 1)

            def out_high(n):
                act.wait_ge(out_ready, c.out + (n + 1))
                tile = bass.ds(c.o_tile, 1)
                for hd in range(2):
                    if n != 1 - hd:
                        rows = slice(hd * HD, (hd + 1) * HD)
                        cols = slice(0, DEC) if n == 2 else slice(DEC, TOK)
                        src = out_ps[rows, hd * DEC:(hd + 1) * DEC] if n == 2 else out_ps[rows, :]
                        last = act.activation(o_hi[rows, tile, cols],
                                              src.rearrange("p (a c) -> p a c", a=1), ACT.Copy)
                last.then_inc(out_hi, 1)

            if not mem:
                act.wait_ge(turned_ready, c.round + 1)
                act.activation(v[par][:, :, :], turned[:, :].rearrange("p (j c) -> p j c", j=QT), ACT.Copy) \
                    .then_inc(turned_free, 1)
            if stick:
                softplus(0)
            if not mem:
                act.wait_ge(turned_ready, c.round + 2)
                act.activation(vn[par][:, :], turned[:, 0:P], ACT.Copy).then_inc(turned_free, 1)
            if not stick:
                exponential(0)
            for u in range(UNITS):
                if c.fill is not None and u % 3 == 0:
                    n = u // 3 + 1
                    high(c.fill_slab + n, (c.fpar + n) % 2)
                if u == 1 and not mem:
                    act.wait_ge(qkv_ready, c.qkv)
                    pair = bass.ds(c.pair, 1)
                    act.dma_start(k_o[layer, pair].rearrange("a p c -> (a p) c"), kb[par][:, PAST:]) \
                        .then_inc(kv_stored, 16)
                    act.dma_start(v_o[layer, pair].rearrange("a p c -> (a p) c"), vf[:, :]) \
                        .then_inc(kv_stored, 16)
                if stick:
                    if u + 1 < UNITS:
                        softplus(u + 1)
                    exponential(u)
                elif u + 1 < UNITS:
                    exponential(u + 1)
                copy_turned(u)
                if u == QT:
                    out_high(0)
            out_high(1)
            out_high(2)

        for layer in range(DEPTH):
            s0 = layer_slab(layer)
            high(s0 + 1, 1)
            root(2 * layer + 1)
            act.preload_act_table_set("natural_log_exp_and_others")
            if layer == 0:
                act.wait_ge(gate_in, 1)
                soft = work_b[0:HEADS, 0, :]
                act.activation(soft, work_a[0:HEADS, 0, :], ACT.Abs)
                act.drain()
                act.activation(soft, soft, ACT.Exp, scale=-1.0)
                act.drain()
                act.activation(soft, soft, ACT.Ln, bias=1.0).then_inc(gate_soft, 1)
                act.wait_ge(cum_made, 1)
                act.dma_start(cum_dram, cum[:, :]).then_inc(cum_out, 16)
                act.dma_start(lf_o, lf[:, PAST:]).then_inc(lf_stored, 16)
            high(s0 + 2, 0)
            if layer == 0:
                act.wait_ge(turned_ready, 2 * DEPTH + 1)
                act.activation(cq[:, :, :], turned[:, 0:QT * HEADS].rearrange("p (i h) -> p i h", i=QT),
                               ACT.Copy)
                for hd in range(2):
                    rows = slice(hd * HD, (hd + 1) * HD)
                    last = act.activation(cq_s[rows, :],
                                          turned[rows, QT * HEADS + hd:(QT + 1) * HEADS:2], ACT.Copy)
                last.then_inc(turned_free, 1)
                act.wait_ge(mem_stored, 16 * MKV_SLABS)
            calls(act, layer, attention)
            for m in range(OUT_TILES):
                high(s0 + IN_TILES + m + 1, (m + 1) % 2)
                split_x(2 * layer + 1, m, 4 + layer)
            sg = gu_slab(layer)
            high(sg + 1, 1)
            root(2 * layer + 2)

            def gate_up(j):
                act.wait_ge(gated, j + (layer * FT + 1))
                act.activation(work_b[:, 0, :], work_a[:, 0, :], ACT.Silu).then_inc(silu_made, 1)
                high(j * 2 + (sg + 2), 0)
                act.wait_ge(prod_made, j + (layer * FT + 1))
                act.activation(f_hi[:, bass.ds(j, 1), :], work_c[:, 0:1, :], ACT.Copy).then_inc(fhi_made, 1)

            act.wait_ge(kv_stored, 32 * PAIRS * (layer + 1))
            gate_up(0)
            with act.Fori(1, FT) as j:
                high(j * 2 + (sg + 1), 1)
                gate_up(j)
            sd = sg + GU_TILES
            for m in range(KT):
                for n in range(3):
                    s = 3 * m + n + 1
                    if layer < DEPTH - 1 or s < 3 * KT:
                        high(sd + s, s % 2, (DOWN_CUTS[s % 3] if s < 3 * KT else KT) * P)
                split_x(2 * layer + 2, m, 1 if layer == 0 else None)
        root(2 * DEPTH + 1)

    @block.vector
    def _(dve):
        def factor(norm, use):
            dve.wait_ge(score_ready, use + 2)
            width = N_MEM if norm == 0 else TOK
            out = rstd[:, 0:width]
            dve.tensor_scalar(halves(out), score[:, :, 0:width // 2], 1.0 / D_MODEL, EPS,
                              ALU.mult, ALU.add).then_inc(mean_ready, 1)
            dve.drain()
            dve.sem_inc(score_free, 2)
            dve.wait_ge(root_ready, norm + 1)
            dve.reciprocal(out, out)
            dve.drain()

        def x_low(norm, m, g):
            dve.wait_ge(xhi_made, KT * norm + m + 1)
            dve.scalar_tensor_tensor(out=xg_lo[:, m, :], in0=x[:, m, :],
                                     scalar=gain[:, g * KT + m:g * KT + m + 1],
                                     in1=xg_hi[:, m, :].bitcast(F32), op0=ALU.mult,
                                     op1=ALU.subtract).then_inc(xlo_made, 1)

        def mem_low(layer):
            for k in range(KT):
                dve.wait_ge(m_hi_made, layer * KT + k + 1)
                c = (2 + layer) * KT + k
                dve.scalar_tensor_tensor(out=m_lo[:, k, :], in0=m_raw[:, k, :], scalar=gain[:, c:c + 1],
                                         in1=m_hi[:, k, :].bitcast(F32), op0=ALU.mult,
                                         op1=ALU.subtract).then_inc(m_lo_made, 1)

        mem_low(0)
        factor(0, 0)
        for s in range(MKV_SLABS):
            if s == MKV_TILES:
                mem_low(1)
            layer, c = divmod(s, MKV_TILES)
            dve.wait_ge(slab_done, s + 1)
            out = mk[:, layer, c, :] if c < 2 else mvt[:, 2 * layer + c - 2, :]
            dve.tensor_tensor(out, acc[:, s % 2, 0, 0:N_MEM], rstd[:, 0:N_MEM], ALU.mult) \
                .then_inc(mem_kv, 1)
            dve.drain()
            dve.sem_inc(acc_free, 1)
            x_low(0, s, 0)

        def tile_out(slab, tpar, outs):
            dve.wait_ge(slab_done, slab + 1)
            for out, rows, scale in outs:
                src = acc[rows, tpar, :, 0:HALF]
                if scale is None:
                    last = dve.tensor_tensor(halves(out), src, halves(rstd[rows, :]), ALU.mult)
                else:
                    last = dve.scalar_tensor_tensor(out=halves(out), in0=src, scalar=scale,
                                                    in1=halves(rstd[rows, :]), op0=ALU.mult, op1=ALU.mult)
            return last

        def queries(slab, tpar, par, scale):
            dve.wait_ge(slab_done, slab + 1)
            for hd in range(2):
                rows, cols = slice(hd * HD, (hd + 1) * HD), slice(hd * DEC, (hd + 1) * DEC)
                dve.scalar_tensor_tensor(out=qs[par][rows, cols], in0=acc[rows, tpar, 0, 0:DEC], scalar=scale,
                                         in1=rstd[rows, 0:DEC], op0=ALU.mult, op1=ALU.mult)
            return tile_out(slab, tpar, [(qz[par][0:HD, 0, :], slice(0, HD), scale),
                                         (qz[par][HD:P, 1, :], slice(HD, P), scale)])

        def attention(c):
            layer, par, mem = c.layer, c.par, c.mem
            fox = layer == 0 and not mem
            stick = layer == 1 and not mem

            def front(u):
                b, w, sample = c.buf(u), c.width(u), u == 2 * QT
                hd, i = divmod(u, QT)
                uses = 2 if sample else 1
                shape = halves if sample else (lambda t: t)
                wide = work_a[:, b, 0:w]
                z = score[:, :, 0:w // 2] if sample else score[:, u % 2, 0:w]
                diag = work_a[:, b, w - (DEC if sample else P):w]

                def mask(const, op):
                    n = DEC if sample else P
                    dve.drain()
                    return dve.tensor_tensor(diag, diag, cst[:, const:const + n], op)

                if stick:
                    dve.wait_ge(probs_ready, c.unit + (u - 1))
                    dve.wait_ge(soft_ready, c.pair * UNITS + (u + 1))
                    tail = work_c[:, b, 0:w]
                    dve.scalar_tensor_tensor(out=shape(wide), in0=z, scalar=0.0, in1=shape(tail),
                                             op0=ALU.max, op1=ALU.add)
                    mask(C_SB1S if sample else C_SB1, ALU.mult)
                    dve.drain()
                    dve.tensor_tensor_scan(tail[:, ::-1], wide[:, ::-1], wide[:, ::-1], 0.0,
                                           ALU.add, ALU.bypass)
                    dve.drain()
                    dve.tensor_tensor(shape(wide), z, shape(tail), ALU.subtract)
                    mask(C_SBNS if sample else C_SBN, ALU.add).then_inc(exp_in, 1)
                    dve.sem_inc(score_free, uses)
                    return
                dve.wait_ge(score_ready, c.use + (u + uses))
                if fox:
                    if sample:
                        dve.wait_ge(cum_in[par], c.cums)
                        gate_q, gate_k = cq_s[:, bass.ds(c.pair, 1)], ckbs[par][:, :]
                    else:
                        if u == 0:
                            dve.wait_ge(cum_in[par], c.cums)
                        gate_q = cq[:, i, bass.ds(c.pair * 2 + hd, 1)]
                        gate_k = ckb[par][:, hd, 0:w]
                    dve.scalar_tensor_tensor(out=shape(wide), in0=z, scalar=gate_q, in1=shape(gate_k),
                                             op0=ALU.subtract, op1=ALU.add)
                    mask(C_FOXS if sample else C_FOX, ALU.add)
                else:
                    dve.tensor_copy(shape(wide), z)
                dve.drain()
                dve.sem_inc(score_free, uses)
                dve.tensor_reduce(least[:, b:b + 1], wide, AX, ALU.min).then_inc(exp_in, 1)

            def normalize(u):
                b, w = c.buf(u), c.width(u)
                dve.wait_ge(exp_out, c.unit + (u + 1))
                dve.reciprocal(inv[:, b:b + 1], total[:, b:b + 1])
                dve.drain()
                dve.tensor_scalar(work_b[:, b, 0:w], work_b[:, b, 0:w], inv[:, b:b + 1], None,
                                  ALU.mult).then_inc(probs_ready, 1)

            def out_low(n):
                dve.wait_ge(out_hi, c.out + (n + 1))
                tile = bass.ds(c.o_tile, 1)
                for hd in range(2):
                    if n != 1 - hd:
                        rows = slice(hd * HD, (hd + 1) * HD)
                        cols = slice(0, DEC) if n == 2 else slice(DEC, TOK)
                        src = out_ps[rows, hd * DEC:(hd + 1) * DEC] if n == 2 else out_ps[rows, :]
                        last = dve.tensor_tensor(o_lo[rows, tile, cols],
                                                 src.rearrange("p (a c) -> p a c", a=1),
                                                 o_hi[rows, tile, cols].bitcast(F32), ALU.subtract)
                last.then_inc(out_free, 1)

            def fill_out(n):
                slab, tpar = c.fill_slab + n, (c.fpar + n) % 2
                if n == 0:
                    last = queries(slab, tpar, c.fpar, -SCALE if layer == 0 else SCALE)
                elif n == 1:
                    last = tile_out(slab, tpar, [(kb[c.fpar][:, PAST:], slice(0, P), None)])
                else:
                    at_least(dve, kv_stored, 0 if mem and layer == 0 else
                             (c.a + (layer * PAIRS - 1)) * 32)
                    last = tile_out(slab, tpar, [(vf[:, :], slice(0, P), None)])
                last.then_inc(qkv_ready, 1)
                dve.drain()
                dve.sem_inc(acc_free, 1)

            front(0)
            for u in range(UNITS):
                if u + 1 < UNITS:
                    front(u + 1)
                if not stick:
                    normalize(u)
                if u == QT:
                    out_low(0)
                if c.fill is not None and u % 3 == 2:
                    fill_out(u // 3)
            out_low(1)
            out_low(2)

        for layer in range(DEPTH):
            s0 = layer_slab(layer)
            factor(2 * layer + 1, LAYER_USE[layer])
            queries(s0, 0, 0, -SCALE).then_inc(qkv_ready, 1)
            dve.drain()
            dve.sem_inc(acc_free, 1)
            if layer == 0:
                y = work_a[0:HEADS, 0, :]
                dve.wait_ge(score_ready, LAYER_USE[layer] + 4)
                dve.tensor_tensor(halves(y), score[0:HEADS, :, 0:HALF], halves(rstd[0:HEADS, :]), ALU.mult)
                dve.drain()
                dve.sem_inc(score_free, 2)
                dve.wait_ge(wf_in, 32)
                dve.tensor_scalar(y, y, bias_f[:, 0:1], None, ALU.add).then_inc(gate_in, 1)
                dve.wait_ge(gate_soft, 1)
                dve.scalar_tensor_tensor(out=lf[:, PAST:], in0=y, scalar=0.0, in1=work_b[0:HEADS, 0, :],
                                         op0=ALU.min, op1=ALU.subtract)
                dve.drain()
                dve.wait_ge(clf_in, 16)
                for c0, c1 in ((0, KEYS_S), (KEYS_S, PAST + TOK)):
                    dve.tensor_tensor_scan(cum[:, c0:c1], lf[:, c0:c1], lf[:, c0:c1], 0.0,
                                           ALU.add, ALU.bypass)
                dve.drain()
                dve.tensor_copy(dup[:, 0:DEC], cum[:, PAST:KEYS_S])
                dve.tensor_copy(dup[:, DEC:P], cum[:, PAST:KEYS_S]).then_inc(cum_made, 1)
            queries(s0 + 1, 1, 1, -SCALE).then_inc(qkv_ready, 1)
            dve.drain()
            dve.sem_inc(acc_free, 1)
            if layer == 0:
                dve.wait_ge(turned_free, 2 * DEPTH + 1)
            calls(dve, layer, attention)

            def residual(slab, m):
                dve.wait_ge(slab_done, slab + 1)
                dve.tensor_tensor(halves(x[:, m, :]), acc[:, m % 2, :, 0:HALF], halves(x[:, m, :]),
                                  ALU.add).then_inc(x_new, 1)
                dve.drain()
                dve.sem_inc(acc_free, 1)

            for m in range(OUT_TILES):
                residual(s0 + IN_TILES + m, m)
                x_low(2 * layer + 1, m, 4 + layer)
            sg = gu_slab(layer)
            factor(2 * layer + 2, attn_use(layer, ATTNS))

            def gate_up(j):
                n = layer * FT + 1
                tile_out(j * 2 + sg, 0, [(work_a[:, 0, :], slice(0, P), None)]).then_inc(gated, 1)
                dve.drain()
                dve.sem_inc(acc_free, 1)
                tile_out(j * 2 + (sg + 1), 1, [(work_c[:, 0, :], slice(0, P), None)])
                dve.drain()
                dve.sem_inc(acc_free, 1)
                dve.wait_ge(silu_made, j + n)
                dve.tensor_tensor(work_c[:, 0, :], work_c[:, 0, :], work_b[:, 0, :], ALU.mult) \
                    .then_inc(prod_made, 1)
                dve.wait_ge(fhi_made, j + n)
                dve.tensor_tensor(f_lo[:, bass.ds(j, 1), :], work_c[:, 0:1, :],
                                  f_hi[:, bass.ds(j, 1), :].bitcast(F32), ALU.subtract).then_inc(flo_made, 1)

            with dve.Fori(0, FT) as j:
                gate_up(j)
            sd = sg + GU_TILES
            for m in range(KT):
                residual(sd + 3 * m + 2, m)
                if layer < DEPTH - 1:
                    x_low(2 * layer + 2, m, 1)
        factor(2 * DEPTH + 1, LAYER_USE[DEPTH])
        for k in range(KT):
            dve.scalar_tensor_tensor(out=x[:, k, :], in0=x[:, k, :],
                                     scalar=gain[:, 6 * KT + k:6 * KT + k + 1], in1=rstd[:, :],
                                     op0=ALU.mult, op1=ALU.mult).then_inc(y_made, 1)

    ctx.close()


def _tiles(w, kt=KT):
    rows, cols = w.shape
    return np.ascontiguousarray(
        w.reshape(kt, P, cols // P, P).transpose(2, 1, 0, 3).reshape(cols // P, P, kt * P))


def _feature_major(a):
    return np.ascontiguousarray(a.T.reshape(-1, P, a.shape[0]).transpose(1, 0, 2))


def _consts():
    q, k = np.arange(P)[:, None], np.arange(P)[None, :]
    qs, ks = np.arange(P)[:, None] % DEC, np.arange(DEC)[None, :]
    out = np.zeros((P, C_END), np.float32)
    out[:, C_ID:C_ID + P] = q == k
    out[:, C_ONES:C_ONES + P] = 1.0
    out[:, C_FOX:C_FOX + P] = np.where(k > q, BIG, 0.0)
    out[:, C_FOXS:C_FOXS + DEC] = np.where(ks > qs, BIG, 0.0)
    out[:, C_SBN:C_SBN + P] = np.where(k >= q, -BIG, 0.0)
    out[:, C_SBNS:C_SBNS + DEC] = np.where(ks >= qs, -BIG, 0.0)
    out[:, C_SB1:C_SB1 + P] = k < q
    out[:, C_SB1S:C_SB1S + DEC] = ks < qs
    return out


def kernel(x_prompt, x_sample, mem_prompt, cache_fox_k, cache_fox_v, cache_fox_logf, cache_sb_k,
           cache_sb_v, cache_mem_k, cache_mem_v, g_mix, w_in_fox, b_f, w_in_sb, g_mem, w_mem_kv,
           w_out, g_ffn, w_gate_up, w_down, g_final):
    import concourse.bacc as bacc
    from concourse.bass_utils import run_bass_kernel_spmd

    A = np.asarray
    W = HEADS * HD
    order = [slice(3 * W, 3 * W + P), slice(3 * W + P, 3 * W + 2 * P)]
    for p in range(PAIRS):
        order += [slice(g * W + p * P, g * W + (p + 1) * P) for g in range(3)]
    fox, stick = A(w_in_fox)[0], A(w_in_sb)[0]
    gate_w = fox[:, 3 * W:3 * W + HEADS]
    fox = np.concatenate([fox[:, :3 * W], fox[:, 3 * W + HEADS:]], axis=1)
    w_in = np.stack([_tiles(np.concatenate([w[:, s] for s in order], axis=1)) for w in (fox, stick)])
    gu = A(w_gate_up)
    gu = gu.reshape(DEPTH, D_MODEL, 2, FT, P).transpose(0, 1, 3, 2, 4).reshape(DEPTH, D_MODEL, 2 * D_FF)
    gains = np.concatenate([A(g_mix), A(g_mem), A(g_ffn), A(g_final)[None]])

    def keys(c):
        return c.reshape(c.shape[0], -1, P).transpose(1, 2, 0)

    def vals(c):
        n = c.shape[0] // P
        return c.reshape(n, P, -1, P).transpose(2, 1, 0, 3).reshape(-1, P, n * P)

    arrays = {
        "x_t": _feature_major(np.concatenate([A(x_sample)[0], A(x_prompt)[0]])),
        "mem_t": _feature_major(A(mem_prompt)[0]),
        "w_mkv": np.stack([_tiles(w) for w in A(w_mem_kv)]),
        "w_in": w_in,
        "w_f": gate_w.reshape(KT, P, HEADS).transpose(1, 0, 2).reshape(P, KT * HEADS),
        "w_out": np.stack([_tiles(w) for w in A(w_out)]),
        "w_gu": np.stack([_tiles(w) for w in gu]),
        "w_dn": np.stack([_tiles(w, FT) for w in A(w_down)]),
        "gains": gains.reshape(7, KT, P).transpose(2, 0, 1).reshape(P, 7 * KT),
        "b_f": A(b_f)[0][:, None],
        "ck": np.stack([keys(A(cache_fox_k)[0, 0]), keys(A(cache_sb_k)[0, 0])]),
        "cv": np.stack([vals(A(cache_fox_v)[0, 0]), vals(A(cache_sb_v)[0, 0])]),
        "clf": A(cache_fox_logf)[0, 0].T,
        "cmk": np.stack([keys(c[0]) for c in A(cache_mem_k)]),
        "cmv": np.stack([vals(c[0]) for c in A(cache_mem_v)]),
        "consts": _consts(),
    }
    outs = {
        "y_t": (P, KT, TOK),
        "k_o": (DEPTH, PAIRS, P, TOK),
        "v_o": (DEPTH, PAIRS, P, TOK),
        "lf_o": (HEADS, TOK),
        "mk_o": (DEPTH, MEM_PAIRS, P, N_MEM),
        "mv_o": (DEPTH, MEM_PAIRS, P, N_MEM),
    }
    nc = bacc.Bacc("TRN2", target_bir_lowering=False, num_devices=1)
    arrays = {n: np.ascontiguousarray(a) for n, a in arrays.items()}
    args = {n: nc.dram_tensor("in_" + n, a.shape, F32, kind="ExternalInput").ap() for n, a in arrays.items()}
    args |= {n: nc.dram_tensor("out_" + n, s, F32, kind="ExternalOutput").ap() for n, s in outs.items()}
    build(nc, **args)
    r = run_bass_kernel_spmd(nc, [{"in_" + n: a for n, a in arrays.items()}], core_ids=[0])
    got = {n: r.results[0]["out_" + n] for n in outs}

    y = got["y_t"].transpose(2, 1, 0).reshape(TOK, D_MODEL)

    def heads(a, part):
        return a[:, :, part].transpose(2, 0, 1).reshape(1, 1, -1, HEADS, HD)

    def mem(a):
        return a.transpose(0, 3, 1, 2).reshape(DEPTH, 1, N_MEM, MEM_HEADS, HD)

    sample, prompt = slice(0, DEC), slice(DEC, TOK)
    out = {}
    for name, part in (("p", prompt), ("s", sample)):
        out[name] = (heads(got["k_o"][0], part), heads(got["v_o"][0], part),
                     got["lf_o"][:, part].T[None, None],
                     heads(got["k_o"][1], part), heads(got["v_o"][1], part))
    result = (y[prompt][None], y[sample][None], *out["p"], mem(got["mk_o"]), mem(got["mv_o"]), *out["s"])
    return tuple(np.ascontiguousarray(a) for a in result)
```

```python
from contextlib import ExitStack

import concourse.bass as bass
import concourse.mybir as mybir
import numpy as np
from concourse.alu_op_type import AluOpType as ALU

F32 = mybir.dt.float32
F32R = mybir.dt.float32r
ACT = mybir.ActivationFunctionType
AX = mybir.AxisListType.X

P = 128
D_MODEL = 1024
SEQ = 512
DEC = 64
PAST = 512
DEPTH = 2
HD = 64
HEADS = 12
N_MEM = 256
MEM_HEADS = 4
D_FF = 2816
EPS = 1e-6
SCALE = HD ** -0.5
BIG = 1e30

TOK = DEC + SEQ
HALF = TOK // 2
KT = D_MODEL // P
FT = D_FF // P
PAIRS = HEADS // 2
MEM_PAIRS = MEM_HEADS // 2
QT = SEQ // P
MB = N_MEM // P
KEYS_S = PAST + DEC
SLAB = KT * P
IN_TILES = 2 + 3 * PAIRS
OUT_TILES = KT
GU_TILES = 2 * FT
DOWN_CUTS = (8, 8, 6)
MKV_TILES = 4

MKV_SLABS = DEPTH * MKV_TILES
LAYER_TILES = IN_TILES + OUT_TILES + GU_TILES + KT
LAYER_SLABS = IN_TILES + OUT_TILES + GU_TILES + 3 * KT
ATTNS = MEM_PAIRS + PAIRS
UNITS = 2 * QT + 1
USES = 2 * QT + 2

C_ID, C_ONES, C_FOX, C_FOXS, C_SBN, C_SBNS, C_SB1, C_SB1S = 0, 128, 256, 384, 448, 576, 640, 768
C_END = 832


def at_least(eng, sem, value):
    if not (isinstance(value, int) and value <= 0):
        eng.wait_ge(sem, value)


def build(nc, x_t, mem_t, w_mkv, w_in, w_f, w_out, w_gu, w_dn, gains, b_f, ck, cv, clf, cmk, cmv,
          consts, y_t, k_o, v_o, lf_o, mk_o, mv_o):
    ctx = ExitStack()
    region = ExitStack()

    def sb(name, shape, dt=F32, stack=ctx):
        return stack.enter_context(nc.sbuf_tensor(name, shape, dt))

    x = sb("x", [P, KT, TOK])
    xg_hi = sb("xg_hi", [P, KT, TOK], F32R)
    xg_lo = sb("xg_lo", [P, KT, TOK], F32R)
    w_raw = sb("w_raw", [P, 2, SLAB])
    w_hi = [sb(f"w_hi{i}", [P, SLAB], F32R) for i in range(2)]
    w_lo = [sb(f"w_lo{i}", [P, SLAB], F32R) for i in range(2)]
    cst = sb("cst", [P, C_END])
    gain = sb("gain", [P, 7 * KT])
    mk = sb("mk", [P, DEPTH, MEM_PAIRS, N_MEM])
    mv = sb("mv", [P, DEPTH, MEM_PAIRS, MB * P])
    rstd = sb("rstd", [P, TOK])
    sumsq = sb("sumsq", [P, TOK])
    work_a = sb("work_a", [P, 2, TOK])
    work_b = sb("work_b", [P, 2, TOK])
    work_c = sb("work_c", [P, 2, TOK])
    least = sb("least", [P, 2])
    total = sb("total", [P, 2])
    inv = sb("inv", [P, 2])
    cq = sb("cq", [P, QT, HEADS])
    cq_s = sb("cq_s", [P, PAIRS])

    at = lambda name, shape, dt=F32: sb(name, shape, dt, region)
    qz = [at(f"qz{i}", [P, 2, TOK]) for i in range(2)]
    qs = [at(f"qs{i}", [P, 2 * DEC]) for i in range(2)]
    kb = [at(f"kb{i}", [P, PAST + TOK]) for i in range(2)]
    vc = [at(f"vc{i}", [P, QT, P]) for i in range(2)]
    v = [at(f"v{i}", [P, QT, P]) for i in range(2)]
    vn = [at(f"vn{i}", [P, P]) for i in range(2)]
    vf_z = at("vf_z", [P, DEC + TOK])
    vf = vf_z[:, DEC:]
    pt = at("pt", [P, QT, SEQ])
    pts = at("pts", [P, QT * P + P])
    gates = at("gates", [P, 2, 2, SEQ])
    ckb = [gates[:, i] for i in range(2)]
    ckbs = [at(f"ckbs{i}", [P, KEYS_S]) for i in range(2)]
    cum = at("cum", [HEADS, PAST + TOK])
    wf_raw = at("wf_raw", [P, KT * HEADS])
    wf_hi = at("wf_hi", [P, KT * HEADS], F32R)
    wf_lo = at("wf_lo", [P, KT * HEADS], F32R)
    bias_f = at("bias_f", [HEADS, 1])
    dup = sb("dup", [HEADS, P], F32, region)
    lf = sb("lf", [HEADS, PAST + TOK], F32, region)
    inner = ExitStack()
    o_hi = sb("o_hi", [P, KT, TOK], F32R, inner)
    o_lo = sb("o_lo", [P, KT, TOK], F32R, inner)
    inner.close()
    m_raw = sb("m_raw", [P, KT, N_MEM], F32, region)
    m_hi = [sb(f"m_hi{i}", [P, KT, N_MEM], F32R, region) for i in range(DEPTH)]
    m_lo = [sb("m_lo", [P, KT, N_MEM], F32R, region)[:, :, :],
            gates[:, :, :, :].bitcast(F32R).rearrange("p a b (k c) -> p (a b k) c", c=N_MEM)]
    region.close()
    f_hi = sb("f_hi", [P, FT, TOK], F32R)
    f_lo = sb("f_lo", [P, FT, TOK], F32R)
    rstd_m = rstd[:, 0:N_MEM]
    mvt = pt[:, :, 0:N_MEM]
    m_sq = pt[:, :, :].rearrange("p j (a c) -> p (j a) c", a=2)

    psum = lambda name, shape: ctx.enter_context(nc.psum_tensor(name, shape, F32))
    acc = psum("acc", [P, 2, 2, 512])
    score = psum("score", [P, 2, 512])
    turned = psum("turned", [P, 512])
    out_ps = psum("out_ps", [P, 512])

    sem = lambda name: ctx.enter_context(nc.semaphore(name))
    const_in = sem("const_in")
    x_in = sem("x_in")
    mem_in = sem("mem_in")
    w_arrived = [sem(f"w_arrived{i}") for i in range(2)]
    whi_made = sem("whi_made")
    wlo_made = sem("wlo_made")
    slab_done = sem("slab_done")
    acc_free = sem("acc_free")
    score_ready = sem("score_ready")
    score_free = sem("score_free")
    exp_in = sem("exp_in")
    exp_out = sem("exp_out")
    probs_ready = sem("probs_ready")
    soft_ready = sem("soft_ready")
    turned_ready = sem("turned_ready")
    turned_free = sem("turned_free")
    out_ready = sem("out_ready")
    out_hi = sem("out_hi")
    out_free = sem("out_free")
    qkv_ready = sem("qkv_ready")
    cache_in = [sem(f"cache_in{i}") for i in range(2)]
    cum_in = [sem(f"cum_in{i}") for i in range(2)]
    kv_stored = sem("kv_stored")
    mem_stored = sem("mem_stored")
    x_new = sem("x_new")
    xhi_made = sem("xhi_made")
    xlo_made = sem("xlo_made")
    sq_made = sem("sq_made")
    sq_added = sem("sq_added")
    mean_ready = sem("mean_ready")
    root_ready = sem("root_ready")
    m_hi_made = sem("m_hi_made")
    m_lo_made = sem("m_lo_made")
    m_sq_made = sem("m_sq_made")
    mem_kv = sem("mem_kv")
    wf_in = sem("wf_in")
    wf_hi_made = sem("wf_hi_made")
    wf_lo_made = sem("wf_lo_made")
    zeroed = sem("zeroed")
    gate_in = sem("gate_in")
    gate_soft = sem("gate_soft")
    lf_made = sem("lf_made")
    cum_made = sem("cum_made")
    clf_in = sem("clf_in")
    lf_stored = sem("lf_stored")
    cum_out = sem("cum_out")
    gated = sem("gated")
    silu_made = sem("silu_made")
    prod_made = sem("prod_made")
    fhi_made = sem("fhi_made")
    flo_made = sem("flo_made")
    y_made = sem("y_made")
    y_stored = sem("y_stored")
    cum_dram = nc.dram_tensor("cum_dram", (HEADS, PAST + TOK), F32).ap()

    ident = cst[:, C_ID:C_ID + P]
    ones = cst[:, C_ONES:C_ONES + P]

    def halves(tile):
        return tile.rearrange("p (h c) -> p h c", h=2)

    def layer_slab(layer):
        return MKV_SLABS + layer * LAYER_SLABS

    def gu_slab(layer):
        return layer_slab(layer) + IN_TILES + OUT_TILES

    def layer_tile(layer):
        return MKV_SLABS + layer * LAYER_TILES

    LAYER_USE = [2, 8 + ATTNS * USES, 12 + 2 * ATTNS * USES]

    def attn_use(layer, a):
        return LAYER_USE[layer] + (4 if layer == 0 else 2) + a * USES

    MEM_ROUNDS = 2 * QT + 1
    PAIR_ROUNDS = 2 + 2 * QT + 2
    LAYER_ROUNDS = MEM_PAIRS * MEM_ROUNDS + PAIRS * PAIR_ROUNDS

    class Call:

        def __init__(self, layer, half, par, mem=False, tiles=(), spread=(0,) * UNITS, fill=0, first=False):
            self.layer, self.par, self.mem = layer, par, mem
            self.a = a = half * 2 + par
            self.stick = layer == 1 and not mem
            self.pair = None if mem else a - MEM_PAIRS
            self.o_tile = PAIRS + a if mem else a - MEM_PAIRS
            self.unit = (a + layer * ATTNS) * UNITS
            self.use = attn_use(layer, a)
            start = 2 * DEPTH + 1 + layer * LAYER_ROUNDS
            self.round = a * MEM_ROUNDS + start if mem else \
                a * PAIR_ROUNDS + (start + MEM_PAIRS * (MEM_ROUNDS - PAIR_ROUNDS))
            self.out = (a + layer * ATTNS) * 3
            self.qkv = layer * IN_TILES + a + 1 if mem else a * 3 + (layer * IN_TILES - 1)
            self.qk = self.qkv if mem or first else self.qkv - 1
            self.caches = (half + (layer * ATTNS // 2 + 1)) * 32
            self.cums = half * 64
            self.tiles = tiles
            self.slabs = [fill * 6 + (layer_slab(layer) + t) for t, _ in tiles]
            self.nums = [fill * 6 + (layer_tile(layer) + t) for t, _ in tiles]
            self.spread = spread
            beside = [u for u, n in enumerate(spread) for _ in range(n)]
            self.per = len(beside) // len(tiles) if tiles else 0
            self.starts = [beside[self.per * n] for n in range(len(tiles))] if beside else []
            self.ends = [beside[self.per * n + self.per - 1] for n in range(len(tiles))] if beside else []

        def buf(self, u):
            return (self.par + u) % 2

        def width(self, u):
            if u == 2 * QT:
                return N_MEM if self.mem else KEYS_S
            return N_MEM if self.mem else (u % QT + 1) * P

        def turned_round(self, u):
            return self.round + (u if self.mem else u + 1 if u == 0 else u + 2)

    def calls(eng, layer, call):
        def pair(half, par, t, fill=0, first=False):
            return Call(layer, half, par, False, [(t + c, "qkv"[c]) for c in range(3)],
                        (3, 3, 2) * 3, fill, first)

        mem0 = Call(layer, 0, 0, True, [(2, "k"), (3, "v")], (2, 2, 2, 2, 2, 2, 2, 1, 1))
        mem1 = Call(layer, 0, 1, True, [(4, "q")], (1, 1, 2, 1, 1, 2, 0, 0, 0))
        pair0 = pair(1, 0, 5, first=True)
        last = Call(layer, ATTNS // 2 - 1, 1, False, [(IN_TILES, "o"), (IN_TILES + 1, "o")],
                    (2, 2, 2, 2, 2, 2, 1, 1, 0))
        call(mem0, None, mem1)
        call(mem1, mem0, pair0)
        call(pair0, mem1, pair(1, 1, 8))
        with eng.Fori(0, (PAIRS - 2) // 2) as i:
            odd, even = pair(i + 1, 1, 8, i), pair(i + 2, 0, 11, i)
            call(odd, pair(i + 1, 0, 5, i), even)
            call(even, odd, pair(i + 2, 1, 14, i))
        call(last, pair(ATTNS // 2 - 1, 0, 5), None)

    block = ctx.enter_context(nc.Block())

    @block.sync
    def _(sp):
        sp.dma_start(m_raw[:, :, :], mem_t).then_inc(mem_in, 16)
        sp.dma_start(gain[:, :], gains).then_inc(const_in, 16)
        sp.dma_start(cst[:, :], consts).then_inc(const_in, 16)

        def slab(s, par, src, cols=SLAB):
            at_least(sp, wlo_made, s - 1)
            sp.dma_start(w_raw[:, par, 0:cols], src).then_inc(w_arrived[par], 16)

        def cache(layer, half, par, mem):
            c = Call(layer, half, par, mem)
            at_least(sp, out_ready, 0 if layer == 0 and mem else c.out - 3)
            if mem:
                sp.dma_start(kb[par][:, 0:N_MEM], cmk[layer, par]).then_inc(cache_in[par], 16)
                sp.dma_start(vc[par][:, 0:MB, :], cmv[layer, par].rearrange("p (j c) -> p j c", j=MB)) \
                    .then_inc(cache_in[par], 16)
                return
            sp.dma_start(kb[par][:, 0:PAST], ck[layer, bass.ds(c.pair, 1)].rearrange("a p c -> (a p) c")) \
                .then_inc(cache_in[par], 16)
            sp.dma_start(vc[par][:, :, :], cv[layer, bass.ds(c.pair, 1)].rearrange("a p (j c) -> (a p) j c", j=QT)) \
                .then_inc(cache_in[par], 16)
            if layer == 0:
                sp.wait_ge(cum_out, 16)
                for hd in range(2):
                    row = cum_dram[bass.ds(c.pair * 2 + hd, 1), :]
                    sp.dma_start(ckb[par][:, hd, :], row[:, KEYS_S:].to_broadcast([P, SEQ])) \
                        .then_inc(cum_in[par], 16)
                    sp.dma_start(ckbs[par][hd * HD:(hd + 1) * HD, :],
                                 row[:, 0:KEYS_S].to_broadcast([HD, KEYS_S])).then_inc(cum_in[par], 16)

        for s in range(2):
            slab(s, s, w_mkv[0, s])
        sp.dma_start(x[:, :, :], x_t).then_inc(x_in, 16)
        sp.dma_start(wf_raw[:, :], w_f).then_inc(wf_in, 16)
        sp.dma_start(bias_f[:, :], b_f).then_inc(wf_in, 16)
        sp.dma_start(lf[:, 0:PAST], clf).then_inc(clf_in, 16)
        for s in range(2, MKV_SLABS):
            slab(s, s % 2, w_mkv[s // MKV_TILES, s % MKV_TILES])
        for layer in range(DEPTH):
            s0 = layer_slab(layer)
            for t in range(2):
                slab(s0 + t, t, w_in[layer, t])
            if layer:
                sp.wait_ge(slab_done, s0)
            cache(layer, 0, 0, True)
            cache(layer, 0, 1, True)
            for t in range(2, 8):
                slab(s0 + t, t % 2, w_in[layer, t])
                if t in (5, 6):
                    cache(layer, 1, t - 5, False)
            with sp.Fori(0, (PAIRS - 2) // 2) as i:
                for par in range(2):
                    for c in range(3):
                        t = 8 + 3 * par + c
                        slab(i * 6 + (s0 + t), t % 2,
                             w_in[layer, bass.ds(i * 6 + t, 1)].rearrange("a p c -> (a p) c"))
                        if c == 1:
                            cache(layer, i + 2, par, False)
            for first, src, count in ((s0 + IN_TILES, w_out, OUT_TILES), (gu_slab(layer), w_gu, GU_TILES)):
                with sp.Fori(0, count // 2) as i:
                    for j in range(2):
                        slab(i * 2 + (first + j), j,
                             src[layer, bass.ds(i * 2 + j, 1)].rearrange("a p c -> (a p) c"))
            with sp.Fori(0, KT // 2) as i:
                for n in range(6):
                    m, c = divmod(n, 3)
                    cols = DOWN_CUTS[c] * P
                    src = w_dn[layer, bass.ds(i * 2 + m, 1)].rearrange("a p c -> (a p) c")
                    slab(i * 6 + (gu_slab(layer) + GU_TILES + n), n % 2,
                         src[:, c * SLAB:c * SLAB + cols], cols)
        for k in range(KT):
            sp.wait_ge(y_made, k + 1)
            sp.dma_start(y_t[:, k, :], x[:, k, :]).then_inc(y_stored, 16)
        sp.wait_ge(y_stored, 16 * KT)
        sp.wait_ge(kv_stored, 32 * DEPTH * PAIRS)
        sp.wait_ge(mem_stored, 16 * MKV_SLABS)
        sp.wait_ge(lf_stored, 16)

    @block.gpsimd
    def _(pool):
        def low(s, par, cols=SLAB):
            pool.wait_ge(whi_made, s + 1)
            pool.tensor_tensor(w_lo[par][:, 0:cols], w_raw[:, par, 0:cols],
                               w_hi[par][:, 0:cols].bitcast(F32), ALU.subtract).then_inc(wlo_made, 1)

        def add_square(norm, m):
            if m:
                if m > 1:
                    pool.wait_ge(sq_added, norm * (KT - 1) + m - 1)
                pool.wait_ge(sq_made, norm * KT + m + 1)
                pool.tensor_tensor(sumsq[:, :], sumsq[:, :], work_c[:, m % 2, :], ALU.add) \
                    .then_inc(sq_added, 1)

        def zero_rows(layer):
            tiles = [vf_z[:, 0:DEC]]
            for par in range(2):
                tiles += [qz[par][HD:P, 0, :], qz[par][0:HD, 1, :], qs[par][HD:P, 0:DEC], qs[par][0:HD, DEC:]]
            for n, tile in enumerate(tiles):
                pool.memset(tile, 0.0).then_inc(zeroed, 1)
                pool.wait_ge(zeroed, len(tiles) * layer + n + 1)

        for s in range(MKV_SLABS):
            low(s, s % 2)
            add_square(0, s)
        pool.wait_ge(wf_hi_made, 1)
        pool.tensor_tensor(wf_lo[:, :], wf_raw[:, :], wf_hi[:, :].bitcast(F32), ALU.subtract) \
            .then_inc(wf_lo_made, 1)
        for layer in range(DEPTH):
            s0 = layer_slab(layer)
            low(s0, 0)
            low(s0 + 1, 1)
            if layer:
                pool.wait_ge(slab_done, s0)
            zero_rows(layer)
            with pool.Fori(1, IN_TILES // 2) as i:
                for j in range(2):
                    low(i * 2 + (s0 + j), j)
            for m in range(OUT_TILES):
                low(s0 + IN_TILES + m, m % 2)
                if m:
                    add_square(2 * layer + 1, m - 1)
            low(gu_slab(layer), 0)
            add_square(2 * layer + 1, KT - 1)
            low(gu_slab(layer) + 1, 1)
            with pool.Fori(1, GU_TILES // 2) as i:
                for j in range(2):
                    low(i * 2 + (gu_slab(layer) + j), j)
            for m in range(KT):
                for c, cut in enumerate(DOWN_CUTS):
                    low(gu_slab(layer) + GU_TILES + 3 * m + c, (3 * m + c) % 2, cut * P)
                if m:
                    add_square(2 * layer + 2, m - 1)
            add_square(2 * layer + 2, KT - 1)

    @block.tensor
    def _(pe):
        def passes(par, k, hi, lo, tpar, first, last):
            width = hi.shape[-1]
            cuts = ((0, HALF), (HALF, TOK)) if width == TOK else ((0, width),)
            parts = ((w_hi, hi), (w_hi, lo), (w_lo, hi))
            for n, (w, a) in enumerate(parts):
                for h, (c0, c1) in enumerate(cuts):
                    mm = pe.matmul(acc[:, tpar, h, 0:c1 - c0], w[par][:, k * P:(k + 1) * P], a[:, c0:c1],
                                   start=first and n == 0, stop=last and n == 2)
            return mm

        def begin(s, t):
            pe.wait_ge(wlo_made, s + 1)
            at_least(pe, acc_free, t - 1)

        def product(s, t, par, tpar, hi, lo, kts=KT, k0=0, first=True, last=True, before=None):
            begin(s, t)
            for k in range(kts):
                if before is not None:
                    before(k0 + k)
                mm = passes(par, k, hi[:, k0 + k, :], lo[:, k0 + k, :], tpar,
                            first and k == 0, last and k == kts - 1)
            mm.then_inc(slab_done, 1)

        def norm_sum(norm, use):
            pe.wait_ge(sq_added, (KT - 1) * (norm + 1))
            pe.wait_ge(score_free, use)
            for h in range(2):
                pe.matmul(score[:, h, 0:HALF], ones, sumsq[:, h * HALF:(h + 1) * HALF],
                          start=True, stop=True).then_inc(score_ready, 1)

        pe.wait_ge(const_in, 32)
        pe.wait_ge(m_sq_made, 1)
        for h in range(2):
            for k in range(KT):
                mm = pe.matmul(score[:, h, 0:P], ones, m_sq[:, k, h * P:(h + 1) * P],
                               start=(k == 0), stop=(k == KT - 1))
            mm.then_inc(score_ready, 1)

        def turn_mem(s):
            n = 2 * (s // MKV_TILES) + s % 2
            pe.wait_ge(mem_kv, s + 1)
            at_least(pe, turned_free, n)
            for j in range(MB):
                mm = pe.transpose(turned[:, j * P:(j + 1) * P], mvt[:, n, j * P:(j + 1) * P], ident)
            mm.then_inc(turned_ready, 1)

        for s in range(MKV_SLABS):
            layer = s // MKV_TILES
            product(s, s, s % 2, s % 2, m_hi[layer], m_lo[layer],
                    before=lambda k: pe.wait_ge(m_lo_made, KT * layer + k + 1))
            if s and (s - 1) % MKV_TILES >= 2:
                turn_mem(s - 1)
        turn_mem(MKV_SLABS - 1)

        def scores(c, u):
            if u == 0:
                pe.wait_ge(qkv_ready, c.qk)
            width = c.width(u)
            if u == 2 * QT:
                pe.wait_ge(cache_in[c.par], c.caches)
                pe.wait_ge(score_free, c.use + u)
                for h in range(2):
                    pe.matmul(score[:, h, 0:width // 2], qs[c.par][:, :],
                              kb[c.par][:, h * width // 2:(h + 1) * width // 2],
                              start=True, stop=True).then_inc(score_ready, 1)
                return
            hd, i = divmod(u, QT)
            keys = mk[:, c.layer, c.par, :] if c.mem else kb[c.par][:, KEYS_S:KEYS_S + width]
            pe.wait_ge(score_free, c.use + (u - 1))
            pe.matmul(score[:, u % 2, 0:width], qz[c.par][:, hd, DEC + i * P:DEC + (i + 1) * P], keys,
                      start=True, stop=True).then_inc(score_ready, 1)

        def turn_blocks(n, tile, blocks):
            pe.wait_ge(turned_free, n)
            for j in range(blocks):
                mm = pe.transpose(turned[:, j * P:(j + 1) * P], tile[:, j * P:(j + 1) * P], ident)
            mm.then_inc(turned_ready, 1)

        def turn(c, u):
            pe.wait_ge(probs_ready, c.unit + (u + 1))
            turn_blocks(c.turned_round(u), work_b[:, c.buf(u), :], c.width(u) // P)

        def turn_rest(c):
            if not c.mem:
                turn_blocks(c.turned_round(2 * QT) + 1,
                            work_b[:, c.buf(2 * QT), KEYS_S - P:KEYS_S], 1)

        def values(c, hd):
            pe.wait_ge(turned_free, c.turned_round(QT * (hd + 1) - 1) + 1)
            at_least(pe, out_free, c.out + hd)
            count = MB if c.mem else QT
            for j in range(count):
                c0 = 0 if c.mem else j * P
                val = mv[:, c.layer, c.par, j * P:(j + 1) * P] if c.mem else v[c.par][:, j, :]
                mm = pe.matmul(out_ps[:, c0:SEQ], val, pt[:, j, c0:SEQ], start=(j == 0),
                               stop=(j == count - 1), skip_group_check=True)
            mm.then_inc(out_ready, 1)

        def values_sample(c):
            pe.wait_ge(turned_free, c.turned_round(2 * QT) + (1 if c.mem else 2))
            pe.wait_ge(out_free, c.out + 2)
            count = MB if c.mem else QT
            for j in range(count):
                mm = pe.matmul(out_ps[:, 0:P], vc[c.par][:, j, :], pts[:, j * P:(j + 1) * P],
                               start=(j == 0), stop=(c.mem and j == count - 1))
            if not c.mem:
                mm = pe.matmul(out_ps[:, 0:P], vn[c.par][:, :], pts[:, QT * P:],
                               start=False, stop=True)
            mm.then_inc(out_ready, 1)

        def attention(c, prev, nxt):
            done = [0]

            def fill(pieces):
                for g in range(done[0], done[0] + pieces):
                    n, k = divmod(g, c.per)
                    slot = c.tiles[n][0] % 2
                    if k == 0:
                        begin(c.slabs[n], c.nums[n])
                    if c.tiles[n][1] == "o":
                        row = (PAIRS, PAIRS + 1, 0, 1, 2, 3, 4)[k]
                        if row == 4:
                            pe.wait_ge(out_free, c.out)
                        passes(slot, row, o_hi[:, row, :], o_lo[:, row, :], slot, k == 0, False)
                    else:
                        mm = passes(slot, k, xg_hi[:, k, :], xg_lo[:, k, :], slot, k == 0, k == KT - 1)
                        if k == KT - 1:
                            mm.then_inc(slab_done, 1)
                done[0] += pieces

            if prev is None:
                scores(c, 0)
                scores(c, 1)
            for u in range(UNITS):
                pieces = c.spread[u]
                half = pieces // 2
                fill(pieces - half)
                if u == 0 and prev is not None:
                    turn(prev, 2 * QT)
                    values(prev, 1)
                    turn_rest(prev)
                if u == 1 and not c.mem:
                    pe.wait_ge(qkv_ready, c.qkv)
                    turn_blocks(c.round, vf[:, DEC:], QT)
                if u == 1 and prev is not None:
                    values_sample(prev)
                if u == 2 and not c.mem:
                    turn_blocks(c.round + 2, vf_z, 1)
                if u == QT + 1:
                    values(c, 0)
                fill(half)
                if u:
                    turn(c, u - 1)
                if u + 2 < UNITS:
                    scores(c, u + 2)
                elif nxt is not None:
                    scores(nxt, u + 2 - UNITS)
            if nxt is None:
                turn(c, 2 * QT)
                values(c, 1)
                turn_rest(c)
                values_sample(c)

        for layer in range(DEPTH):
            s0, t0 = layer_slab(layer), layer_tile(layer)
            product(s0, t0, 0, 0, xg_hi, xg_lo,
                    before=lambda k: pe.wait_ge(xlo_made, KT * 2 * layer + k + 1))
            norm_sum(2 * layer, LAYER_USE[layer])
            if layer == 0:
                pe.wait_ge(wf_lo_made, 1)
                pe.wait_ge(score_free, LAYER_USE[layer] + 2)
                for h in range(2):
                    for k in range(KT):
                        parts = ((wf_hi, xg_hi), (wf_hi, xg_lo), (wf_lo, xg_hi))
                        for n, (w, a) in enumerate(parts):
                            mm = pe.matmul(score[0:HEADS, h, 0:HALF], w[:, k * HEADS:(k + 1) * HEADS],
                                           a[:, k, h * HALF:(h + 1) * HALF],
                                           start=(k == 0 and n == 0), stop=(k == KT - 1 and n == 2))
                    mm.then_inc(score_ready, 1)
            product(s0 + 1, t0 + 1, 1, 1, xg_hi, xg_lo)
            if layer == 0:
                pe.wait_ge(cum_made, 1)
                pe.wait_ge(turned_free, 2 * DEPTH)
                for i in range(QT):
                    pe.transpose(turned[:, i * HEADS:(i + 1) * HEADS],
                                 cum[:, KEYS_S + i * P:KEYS_S + (i + 1) * P], ident[0:HEADS, 0:HEADS])
                pe.transpose(turned[:, QT * HEADS:(QT + 1) * HEADS], dup[:, :],
                             ident[0:HEADS, 0:HEADS]).then_inc(turned_ready, 1)
            pe.wait_ge(zeroed, 9 * (layer + 1))
            calls(pe, layer, attention)

            so, to = s0 + IN_TILES, t0 + IN_TILES
            pe.wait_ge(out_free, 3 * ATTNS * (layer + 1))
            for n in range(2):
                passes(n, PAIRS - 1, o_hi[:, PAIRS - 1, :], o_lo[:, PAIRS - 1, :], n, False, True) \
                    .then_inc(slab_done, 1)
            with pe.Fori(1, OUT_TILES // 2) as i:
                for j in range(2):
                    product(i * 2 + (so + j), i * 2 + (to + j), j, j, o_hi, o_lo)

            sg, tg = so + OUT_TILES, to + OUT_TILES
            product(sg, tg, 0, 0, xg_hi, xg_lo,
                    before=lambda k: pe.wait_ge(xlo_made, KT * (2 * layer + 1) + k + 1))
            norm_sum(2 * layer + 1, attn_use(layer, ATTNS))
            product(sg + 1, tg + 1, 1, 1, xg_hi, xg_lo)
            with pe.Fori(1, GU_TILES // 2) as i:
                for j in range(2):
                    product(i * 2 + (sg + j), i * 2 + (tg + j), j, j, xg_hi, xg_lo)

            sd, td = sg + GU_TILES, tg + GU_TILES

            def down(i, m, before=None):
                k0 = 0
                for n, cut in enumerate(DOWN_CUTS):
                    product(i * 6 + (sd + 3 * m + n), i * 2 + (td + m), (3 * m + n) % 2, m, f_hi, f_lo, cut, k0,
                            n == 0, n == len(DOWN_CUTS) - 1, before)
                    k0 += cut

            down(0, 0, lambda k: pe.wait_ge(flo_made, layer * FT + k + 1))
            down(0, 1)
            with pe.Fori(1, KT // 2) as i:
                down(i, 0)
                down(i, 1)
        norm_sum(2 * DEPTH, LAYER_USE[DEPTH])

    @block.scalar
    def _(act):
        def high(s, par, cols=SLAB):
            act.wait_ge(w_arrived[par], (s - par) * 8 + 16)
            at_least(act, slab_done, s - 1)
            act.activation(w_hi[par][:, 0:cols], w_raw[:, par, 0:cols], ACT.Copy).then_inc(whi_made, 1)

        def root(norm):
            act.wait_ge(mean_ready, norm + 1)
            width = N_MEM if norm == 0 else TOK
            act.activation(rstd[:, 0:width], rstd[:, 0:width], ACT.Sqrt).then_inc(root_ready, 1)

        def split_x(norm, m, g):
            if norm:
                act.wait_ge(x_new, KT * (norm - 1) + m + 1)
            if g is not None:
                act.activation(xg_hi[:, m, :], x[:, m, :], ACT.Copy,
                               scale=gain[:, g * KT + m:g * KT + m + 1]).then_inc(xhi_made, 1)
            if m > 2:
                act.wait_ge(sq_added, (KT - 1) * norm + m - 2)
            square = sumsq[:, :] if m == 0 else work_c[:, m % 2, :]
            act.activation(square, x[:, m, :], ACT.Square).then_inc(sq_made, 1)

        high(0, 0)
        act.wait_ge(const_in, 32)
        act.wait_ge(mem_in, 16)
        act.activation(m_sq[:, :, :], m_raw[:, :, :], ACT.Square).then_inc(m_sq_made, 1)

        def split_mem(layer):
            for k in range(KT):
                c = (2 + layer) * KT + k
                act.activation(m_hi[layer][:, k, :], m_raw[:, k, :], ACT.Copy, scale=gain[:, c:c + 1]) \
                    .then_inc(m_hi_made, 1)

        split_mem(0)
        high(1, 1)
        root(0)
        split_mem(1)
        act.wait_ge(x_in, 16)

        def copy_mem(s):
            n = 2 * (s // MKV_TILES) + s % 2
            act.wait_ge(turned_ready, n + 1)
            act.activation(mv[:, s // MKV_TILES, s % 2, :], turned[:, 0:N_MEM], ACT.Copy) \
                .then_inc(turned_free, 1)

        for s in range(MKV_SLABS):
            if s:
                high(s + 1, (s + 1) % 2)
            split_x(0, s, 0)
            layer, c = divmod(s, MKV_TILES)
            act.wait_ge(mem_kv, s + 1)
            source = mk[:, layer, c, :] if c < 2 else mvt[:, 2 * layer + c - 2, :]
            act.dma_start((mk_o if c < 2 else mv_o)[layer, c % 2], source).then_inc(mem_stored, 16)
            if s and (s - 1) % MKV_TILES >= 2:
                copy_mem(s - 1)
        copy_mem(MKV_SLABS - 1)
        act.wait_ge(wf_in, 32)
        act.activation(wf_hi[:, :], wf_raw[:, :], ACT.Copy).then_inc(wf_hi_made, 1)

        def softplus(c, u):
            b, w = c.buf(u), c.width(u)
            if u == 2 * QT:
                act.wait_ge(score_ready, c.use + (u + 2))
                z, out = score[:, :, 0:HALF], halves(work_c[:, b, :])
            else:
                act.wait_ge(score_ready, c.use + (u + 1))
                z, out = score[:, u % 2, 0:w], work_c[:, b, 0:w]
            act.activation(out, z, ACT.Abs)
            act.drain()
            flat = work_c[:, b, 0:w]
            act.activation(flat, flat, ACT.Exp, scale=-1.0)
            act.drain()
            act.activation(flat, flat, ACT.Ln, bias=1.0).then_inc(soft_ready, 1)

        def exponential(c, u):
            b, w = c.buf(u), c.width(u)
            act.wait_ge(exp_in, c.unit + (u + 1))
            if c.stick:
                act.activation(work_b[:, b, 0:w], work_a[:, b, 0:w], ACT.Exp).then_inc(probs_ready, 1)
            else:
                act.activation(work_b[:, b, 0:w], work_a[:, b, 0:w], ACT.Exp, bias=least[:, b:b + 1],
                               scale=-1.0, accum_out=total[:, b:b + 1]).then_inc(exp_out, 1)

        def copy_round(n, out, src):
            act.wait_ge(turned_ready, n + 1)
            act.activation(out, src, ACT.Copy).then_inc(turned_free, 1)

        def copy_turned(c, u):
            n = c.width(u) // P
            if u < 2 * QT:
                i = u % QT
                copy_round(c.turned_round(u), pt[:, 0:n, i * P:(i + 1) * P],
                           turned[:, 0:n * P].rearrange("p (j q) -> p j q", j=n))
                return
            copy_round(c.turned_round(u), pts[:, 0:n * P], turned[:, 0:n * P])
            if not c.mem:
                copy_round(c.turned_round(u) + 1, pts[:, QT * P:], turned[:, 0:P])

        def out_high(c, n):
            act.wait_ge(out_ready, c.out + (n + 1))
            tile = bass.ds(c.o_tile, 1)
            for hd in range(2):
                if n != 1 - hd:
                    rows = slice(hd * HD, (hd + 1) * HD)
                    cols = slice(0, DEC) if n == 2 else slice(DEC, TOK)
                    src = out_ps[rows, hd * DEC:(hd + 1) * DEC] if n == 2 else out_ps[rows, :]
                    last = act.activation(o_hi[rows, tile, cols],
                                          src.rearrange("p (a c) -> p a c", a=1), ACT.Copy)
            last.then_inc(out_hi, 1)

        def attention(c, prev, nxt):
            if prev is None and c.stick:
                softplus(c, 0)
            for u in range(UNITS):
                if u in c.starts:
                    n = c.starts.index(u)
                    if c.tiles[n][0] != IN_TILES + 1:
                        high(c.slabs[n] + 1, (c.tiles[n][0] + 1) % 2)
                if c.stick and u + 1 < UNITS:
                    softplus(c, u + 1)
                if u + 1 == UNITS and nxt is not None and nxt.stick:
                    softplus(nxt, 0)
                exponential(c, u)
                if u == 0 and prev is not None:
                    copy_turned(prev, 2 * QT)
                    out_high(prev, 1)
                if u == 1 and not c.mem:
                    copy_round(c.round, v[c.par][:, :, :], turned[:, :].rearrange("p (j c) -> p j c", j=QT))
                if u == 2 and not c.mem:
                    copy_round(c.round + 2, vn[c.par][:, :], turned[:, 0:P])
                if u:
                    copy_turned(c, u - 1)
                if u == 1 and prev is not None:
                    out_high(prev, 2)
                if u == QT + 1:
                    out_high(c, 0)
                if u == 1 and not c.mem:
                    act.wait_ge(qkv_ready, c.qkv)
                    pair = bass.ds(c.pair, 1)
                    act.dma_start(k_o[c.layer, pair].rearrange("a p c -> (a p) c"), kb[c.par][:, PAST:]) \
                        .then_inc(kv_stored, 16)
                    act.dma_start(v_o[c.layer, pair].rearrange("a p c -> (a p) c"), vf[:, :]) \
                        .then_inc(kv_stored, 16)
            if nxt is None:
                copy_turned(c, 2 * QT)
                out_high(c, 1)
                out_high(c, 2)

        for layer in range(DEPTH):
            s0 = layer_slab(layer)
            if layer == 0:
                high(s0 + 1, 1)
            high(s0 + 2, 0)
            root(2 * layer + 1)
            act.preload_act_table_set("natural_log_exp_and_others")
            if layer == 0:
                act.wait_ge(gate_in, 1)
                soft = work_b[0:HEADS, 0, :]
                act.activation(soft, work_a[0:HEADS, 0, :], ACT.Abs)
                act.drain()
                act.activation(soft, soft, ACT.Exp, scale=-1.0)
                act.drain()
                act.activation(soft, soft, ACT.Ln, bias=1.0).then_inc(gate_soft, 1)
                act.wait_ge(cum_made, 1)
                act.dma_start(cum_dram, cum[:, :]).then_inc(cum_out, 16)
                act.dma_start(lf_o, lf[:, PAST:]).then_inc(lf_stored, 16)
            if layer == 0:
                act.wait_ge(turned_ready, 2 * DEPTH + 1)
                act.activation(cq[:, :, :], turned[:, 0:QT * HEADS].rearrange("p (i h) -> p i h", i=QT),
                               ACT.Copy)
                for hd in range(2):
                    rows = slice(hd * HD, (hd + 1) * HD)
                    last = act.activation(cq_s[rows, :],
                                          turned[rows, QT * HEADS + hd:(QT + 1) * HEADS:2], ACT.Copy)
                last.then_inc(turned_free, 1)
                act.wait_ge(mem_stored, 16 * MKV_SLABS)
            calls(act, layer, attention)
            for m in range(OUT_TILES):
                high(s0 + IN_TILES + m + 2, m % 2)
                split_x(2 * layer + 1, m, 4 + layer)
            sg = gu_slab(layer)

            def gate_up(j, first=False):
                n = j + (layer * FT + 1)
                high(j * 2 + (sg + 2), 0)
                if first:
                    root(2 * layer + 2)
                act.wait_ge(gated, n)
                act.activation(work_b[:, 0, :], work_a[:, 0, :], ACT.Silu).then_inc(silu_made, 1)
                high(j * 2 + (sg + 3), 1)
                act.wait_ge(prod_made, n)
                act.activation(f_hi[:, bass.ds(j, 1), :], work_c[:, 0:1, :], ACT.Copy).then_inc(fhi_made, 1)

            act.wait_ge(kv_stored, 32 * PAIRS * (layer + 1))
            gate_up(0, True)
            with act.Fori(1, FT) as j:
                gate_up(j)
            sd = sg + GU_TILES
            for m in range(KT):
                for s in range(3 * m + 2, 3 * m + 5):
                    if s < 3 * KT or layer < DEPTH - 1:
                        high(sd + s, s % 2, (DOWN_CUTS[s % 3] if s < 3 * KT else KT) * P)
                split_x(2 * layer + 2, m, 1 if layer == 0 else None)
        root(2 * DEPTH + 1)

    @block.vector
    def _(dve):
        def factor(norm, use):
            dve.wait_ge(score_ready, use + 2)
            width = N_MEM if norm == 0 else TOK
            out = rstd[:, 0:width]
            dve.tensor_scalar(halves(out), score[:, :, 0:width // 2], 1.0 / D_MODEL, EPS,
                              ALU.mult, ALU.add).then_inc(mean_ready, 1)
            dve.drain()
            dve.sem_inc(score_free, 2)
            dve.wait_ge(root_ready, norm + 1)
            dve.reciprocal(out, out)
            dve.drain()

        def x_low(norm, m, g):
            dve.wait_ge(xhi_made, KT * norm + m + 1)
            dve.scalar_tensor_tensor(out=xg_lo[:, m, :], in0=x[:, m, :],
                                     scalar=gain[:, g * KT + m:g * KT + m + 1],
                                     in1=xg_hi[:, m, :].bitcast(F32), op0=ALU.mult,
                                     op1=ALU.subtract).then_inc(xlo_made, 1)

        def mem_low(layer):
            for k in range(KT):
                dve.wait_ge(m_hi_made, layer * KT + k + 1)
                c = (2 + layer) * KT + k
                dve.scalar_tensor_tensor(out=m_lo[layer][:, k, :], in0=m_raw[:, k, :], scalar=gain[:, c:c + 1],
                                         in1=m_hi[layer][:, k, :].bitcast(F32), op0=ALU.mult,
                                         op1=ALU.subtract).then_inc(m_lo_made, 1)

        mem_low(0)
        factor(0, 0)
        for s in range(MKV_SLABS):
            if s == 1:
                mem_low(1)
            layer, c = divmod(s, MKV_TILES)
            dve.wait_ge(slab_done, s + 1)
            out = mk[:, layer, c, :] if c < 2 else mvt[:, 2 * layer + c - 2, :]
            dve.tensor_tensor(out, acc[:, s % 2, 0, 0:N_MEM], rstd[:, 0:N_MEM], ALU.mult) \
                .then_inc(mem_kv, 1)
            dve.drain()
            dve.sem_inc(acc_free, 1)
            x_low(0, s, 0)

        def tile_out(slab, tpar, outs):
            dve.wait_ge(slab_done, slab + 1)
            for out, rows, scale in outs:
                src = acc[rows, tpar, :, 0:HALF]
                if scale is None:
                    last = dve.tensor_tensor(halves(out), src, halves(rstd[rows, :]), ALU.mult)
                else:
                    last = dve.scalar_tensor_tensor(out=halves(out), in0=src, scalar=scale,
                                                    in1=halves(rstd[rows, :]), op0=ALU.mult, op1=ALU.mult)
            return last

        def queries(slab, tpar, par, scale):
            dve.wait_ge(slab_done, slab + 1)
            for hd in range(2):
                rows, cols = slice(hd * HD, (hd + 1) * HD), slice(hd * DEC, (hd + 1) * DEC)
                dve.scalar_tensor_tensor(out=qs[par][rows, cols], in0=acc[rows, tpar, 0, 0:DEC], scalar=scale,
                                         in1=rstd[rows, 0:DEC], op0=ALU.mult, op1=ALU.mult)
            return tile_out(slab, tpar, [(qz[par][0:HD, 0, :], slice(0, HD), scale),
                                         (qz[par][HD:P, 1, :], slice(HD, P), scale)])

        def front(c, u):
            b, w, sample = c.buf(u), c.width(u), u == 2 * QT
            hd, i = divmod(u, QT)
            uses = 2 if sample else 1
            shape = halves if sample else (lambda t: t)
            wide = work_a[:, b, 0:w]
            z = score[:, :, 0:w // 2] if sample else score[:, u % 2, 0:w]
            diag = work_a[:, b, w - (DEC if sample else P):w]

            def mask(const, op):
                n = DEC if sample else P
                dve.drain()
                return dve.tensor_tensor(diag, diag, cst[:, const:const + n], op)

            if c.stick:
                dve.wait_ge(probs_ready, c.unit + (u - 1))
                dve.wait_ge(soft_ready, c.pair * UNITS + (u + 1))
                tail = work_c[:, b, 0:w]
                dve.scalar_tensor_tensor(out=shape(wide), in0=z, scalar=0.0, in1=shape(tail),
                                         op0=ALU.max, op1=ALU.add)
                mask(C_SB1S if sample else C_SB1, ALU.mult)
                dve.drain()
                dve.tensor_tensor_scan(tail[:, ::-1], wide[:, ::-1], wide[:, ::-1], 0.0,
                                       ALU.add, ALU.bypass)
                dve.drain()
                dve.tensor_tensor(shape(wide), z, shape(tail), ALU.subtract)
                mask(C_SBNS if sample else C_SBN, ALU.add).then_inc(exp_in, 1)
                dve.sem_inc(score_free, uses)
                return
            dve.wait_ge(score_ready, c.use + (u + uses))
            if c.mem:
                dve.tensor_copy(shape(wide), z)
            else:
                if u == 0:
                    dve.wait_ge(cum_in[c.par], c.cums)
                if sample:
                    gate_q, gate_k = cq_s[:, bass.ds(c.pair, 1)], ckbs[c.par][:, :]
                else:
                    gate_q, gate_k = cq[:, i, bass.ds(c.pair * 2 + hd, 1)], ckb[c.par][:, hd, 0:w]
                dve.scalar_tensor_tensor(out=shape(wide), in0=z, scalar=gate_q, in1=shape(gate_k),
                                         op0=ALU.subtract, op1=ALU.add)
                mask(C_FOXS if sample else C_FOX, ALU.add)
            dve.drain()
            dve.sem_inc(score_free, uses)
            dve.tensor_reduce(least[:, b:b + 1], wide, AX, ALU.min).then_inc(exp_in, 1)

        def normalize(c, u):
            b, w = c.buf(u), c.width(u)
            dve.wait_ge(exp_out, c.unit + (u + 1))
            dve.reciprocal(inv[:, b:b + 1], total[:, b:b + 1])
            dve.drain()
            dve.tensor_scalar(work_b[:, b, 0:w], work_b[:, b, 0:w], inv[:, b:b + 1], None,
                              ALU.mult).then_inc(probs_ready, 1)

        def out_low(c, n):
            dve.wait_ge(out_hi, c.out + (n + 1))
            tile = bass.ds(c.o_tile, 1)
            for hd in range(2):
                if n != 1 - hd:
                    rows = slice(hd * HD, (hd + 1) * HD)
                    cols = slice(0, DEC) if n == 2 else slice(DEC, TOK)
                    src = out_ps[rows, hd * DEC:(hd + 1) * DEC] if n == 2 else out_ps[rows, :]
                    last = dve.tensor_tensor(o_lo[rows, tile, cols],
                                             src.rearrange("p (a c) -> p a c", a=1),
                                             o_hi[rows, tile, cols].bitcast(F32), ALU.subtract)
            last.then_inc(out_free, 1)

        def fill_out(c, n):
            (t, what), slab = c.tiles[n], c.slabs[n]
            par = 0 if c.mem else 1 - c.par
            if what == "q":
                last = queries(slab, t % 2, par, -SCALE if c.layer == 0 else SCALE)
            elif what == "k":
                last = tile_out(slab, t % 2, [(kb[par][:, PAST:], slice(0, P), None)])
            else:
                if not c.mem:
                    dve.wait_ge(kv_stored, (c.a + (c.layer * PAIRS - 1)) * 32)
                else:
                    at_least(dve, kv_stored, c.layer * PAIRS * 32)
                last = tile_out(slab, t % 2, [(vf[:, :], slice(0, P), None)])
            last.then_inc(qkv_ready, 1)
            dve.drain()
            dve.sem_inc(acc_free, 1)

        def attention(c, prev, nxt):
            if prev is None:
                front(c, 0)
            for u in range(UNITS):
                early = u + 1 == UNITS and nxt is not None and nxt.stick and not c.stick
                if early:
                    normalize(c, u)
                if u + 1 < UNITS:
                    front(c, u + 1)
                elif nxt is not None:
                    front(nxt, 0)
                if not c.stick and not early:
                    normalize(c, u)
                if u < 2 and prev is not None:
                    out_low(prev, u + 1)
                if u == QT + 1:
                    out_low(c, 0)
                if u in c.ends and c.tiles[0][1] != "o":
                    fill_out(c, c.ends.index(u))
            if nxt is None:
                out_low(c, 1)
                out_low(c, 2)

        for layer in range(DEPTH):
            s0 = layer_slab(layer)
            factor(2 * layer + 1, LAYER_USE[layer])
            queries(s0, 0, 0, -SCALE).then_inc(qkv_ready, 1)
            dve.drain()
            dve.sem_inc(acc_free, 1)
            if layer == 0:
                y = work_a[0:HEADS, 0, :]
                dve.wait_ge(score_ready, LAYER_USE[layer] + 4)
                dve.tensor_tensor(halves(y), score[0:HEADS, :, 0:HALF], halves(rstd[0:HEADS, :]), ALU.mult)
                dve.drain()
                dve.sem_inc(score_free, 2)
                dve.wait_ge(wf_in, 32)
                dve.tensor_scalar(y, y, bias_f[:, 0:1], None, ALU.add).then_inc(gate_in, 1)
                dve.wait_ge(gate_soft, 1)
                dve.scalar_tensor_tensor(out=lf[:, PAST:], in0=y, scalar=0.0, in1=work_b[0:HEADS, 0, :],
                                         op0=ALU.min, op1=ALU.subtract)
                dve.drain()
                dve.wait_ge(clf_in, 16)
                for c0, c1 in ((0, KEYS_S), (KEYS_S, PAST + TOK)):
                    dve.tensor_tensor_scan(cum[:, c0:c1], lf[:, c0:c1], lf[:, c0:c1], 0.0,
                                           ALU.add, ALU.bypass)
                dve.drain()
                dve.tensor_copy(dup[:, 0:DEC], cum[:, PAST:KEYS_S])
                dve.tensor_copy(dup[:, DEC:P], cum[:, PAST:KEYS_S]).then_inc(cum_made, 1)
            queries(s0 + 1, 1, 1, -SCALE).then_inc(qkv_ready, 1)
            dve.drain()
            dve.sem_inc(acc_free, 1)
            if layer == 0:
                dve.wait_ge(turned_free, 2 * DEPTH + 1)
            calls(dve, layer, attention)

            def residual(slab, m):
                dve.wait_ge(slab_done, slab + 1)
                dve.tensor_tensor(halves(x[:, m, :]), acc[:, m % 2, :, 0:HALF], halves(x[:, m, :]),
                                  ALU.add).then_inc(x_new, 1)
                dve.drain()
                dve.sem_inc(acc_free, 1)

            for m in range(OUT_TILES):
                residual(s0 + IN_TILES + m, m)
                x_low(2 * layer + 1, m, 4 + layer)
            sg = gu_slab(layer)
            factor(2 * layer + 2, attn_use(layer, ATTNS))

            def gate_up(j):
                n = layer * FT + 1
                tile_out(j * 2 + sg, 0, [(work_a[:, 0, :], slice(0, P), None)]).then_inc(gated, 1)
                dve.drain()
                dve.sem_inc(acc_free, 1)
                tile_out(j * 2 + (sg + 1), 1, [(work_c[:, 0, :], slice(0, P), None)])
                dve.drain()
                dve.sem_inc(acc_free, 1)
                dve.wait_ge(silu_made, j + n)
                dve.tensor_tensor(work_c[:, 0, :], work_c[:, 0, :], work_b[:, 0, :], ALU.mult) \
                    .then_inc(prod_made, 1)
                dve.wait_ge(fhi_made, j + n)
                dve.tensor_tensor(f_lo[:, bass.ds(j, 1), :], work_c[:, 0:1, :],
                                  f_hi[:, bass.ds(j, 1), :].bitcast(F32), ALU.subtract).then_inc(flo_made, 1)

            with dve.Fori(0, FT) as j:
                gate_up(j)
            sd = sg + GU_TILES
            for m in range(KT):
                residual(sd + 3 * m + 2, m)
                if layer < DEPTH - 1:
                    x_low(2 * layer + 2, m, 1)
        factor(2 * DEPTH + 1, LAYER_USE[DEPTH])
        for k in range(KT):
            dve.scalar_tensor_tensor(out=x[:, k, :], in0=x[:, k, :],
                                     scalar=gain[:, 6 * KT + k:6 * KT + k + 1], in1=rstd[:, :],
                                     op0=ALU.mult, op1=ALU.mult).then_inc(y_made, 1)

    ctx.close()


def _tiles(w, kt=KT):
    rows, cols = w.shape
    return np.ascontiguousarray(
        w.reshape(kt, P, cols // P, P).transpose(2, 1, 0, 3).reshape(cols // P, P, kt * P))


def _feature_major(a):
    return np.ascontiguousarray(a.T.reshape(-1, P, a.shape[0]).transpose(1, 0, 2))


def _consts():
    q, k = np.arange(P)[:, None], np.arange(P)[None, :]
    qs, ks = np.arange(P)[:, None] % DEC, np.arange(DEC)[None, :]
    out = np.zeros((P, C_END), np.float32)
    out[:, C_ID:C_ID + P] = q == k
    out[:, C_ONES:C_ONES + P] = 1.0
    out[:, C_FOX:C_FOX + P] = np.where(k > q, BIG, 0.0)
    out[:, C_FOXS:C_FOXS + DEC] = np.where(ks > qs, BIG, 0.0)
    out[:, C_SBN:C_SBN + P] = np.where(k >= q, -BIG, 0.0)
    out[:, C_SBNS:C_SBNS + DEC] = np.where(ks >= qs, -BIG, 0.0)
    out[:, C_SB1:C_SB1 + P] = k < q
    out[:, C_SB1S:C_SB1S + DEC] = ks < qs
    return out


def kernel(x_prompt, x_sample, mem_prompt, cache_fox_k, cache_fox_v, cache_fox_logf, cache_sb_k,
           cache_sb_v, cache_mem_k, cache_mem_v, g_mix, w_in_fox, b_f, w_in_sb, g_mem, w_mem_kv,
           w_out, g_ffn, w_gate_up, w_down, g_final):
    import concourse.bacc as bacc
    from concourse.bass_utils import run_bass_kernel_spmd

    A = np.asarray
    W = HEADS * HD
    order = [slice(3 * W, 3 * W + P), slice(3 * W + P, 3 * W + 2 * P)]
    for p in range(PAIRS):
        order += [slice(g * W + p * P, g * W + (p + 1) * P) for g in ((0, 1, 2) if p else (1, 2, 0))]
    fox, stick = A(w_in_fox)[0], A(w_in_sb)[0]
    gate_w = fox[:, 3 * W:3 * W + HEADS]
    fox = np.concatenate([fox[:, :3 * W], fox[:, 3 * W + HEADS:]], axis=1)
    w_in = np.stack([_tiles(np.concatenate([w[:, s] for s in order], axis=1)) for w in (fox, stick)])
    gu = A(w_gate_up)
    gu = gu.reshape(DEPTH, D_MODEL, 2, FT, P).transpose(0, 1, 3, 2, 4).reshape(DEPTH, D_MODEL, 2 * D_FF)
    gains = np.concatenate([A(g_mix), A(g_mem), A(g_ffn), A(g_final)[None]])

    def keys(c):
        return c.reshape(c.shape[0], -1, P).transpose(1, 2, 0)

    def vals(c):
        n = c.shape[0] // P
        return c.reshape(n, P, -1, P).transpose(2, 1, 0, 3).reshape(-1, P, n * P)

    arrays = {
        "x_t": _feature_major(np.concatenate([A(x_sample)[0], A(x_prompt)[0]])),
        "mem_t": _feature_major(A(mem_prompt)[0]),
        "w_mkv": np.stack([_tiles(w) for w in A(w_mem_kv)]),
        "w_in": w_in,
        "w_f": gate_w.reshape(KT, P, HEADS).transpose(1, 0, 2).reshape(P, KT * HEADS),
        "w_out": np.stack([_tiles(w) for w in A(w_out)]),
        "w_gu": np.stack([_tiles(w) for w in gu]),
        "w_dn": np.stack([_tiles(w, FT) for w in A(w_down)]),
        "gains": gains.reshape(7, KT, P).transpose(2, 0, 1).reshape(P, 7 * KT),
        "b_f": A(b_f)[0][:, None],
        "ck": np.stack([keys(A(cache_fox_k)[0, 0]), keys(A(cache_sb_k)[0, 0])]),
        "cv": np.stack([vals(A(cache_fox_v)[0, 0]), vals(A(cache_sb_v)[0, 0])]),
        "clf": A(cache_fox_logf)[0, 0].T,
        "cmk": np.stack([keys(c[0]) for c in A(cache_mem_k)]),
        "cmv": np.stack([vals(c[0]) for c in A(cache_mem_v)]),
        "consts": _consts(),
    }
    outs = {
        "y_t": (P, KT, TOK),
        "k_o": (DEPTH, PAIRS, P, TOK),
        "v_o": (DEPTH, PAIRS, P, TOK),
        "lf_o": (HEADS, TOK),
        "mk_o": (DEPTH, MEM_PAIRS, P, N_MEM),
        "mv_o": (DEPTH, MEM_PAIRS, P, N_MEM),
    }
    nc = bacc.Bacc("TRN2", target_bir_lowering=False, num_devices=1)
    arrays = {n: np.ascontiguousarray(a) for n, a in arrays.items()}
    args = {n: nc.dram_tensor("in_" + n, a.shape, F32, kind="ExternalInput").ap() for n, a in arrays.items()}
    args |= {n: nc.dram_tensor("out_" + n, s, F32, kind="ExternalOutput").ap() for n, s in outs.items()}
    build(nc, **args)
    r = run_bass_kernel_spmd(nc, [{"in_" + n: a for n, a in arrays.items()}], core_ids=[0])
    got = {n: r.results[0]["out_" + n] for n in outs}

    y = got["y_t"].transpose(2, 1, 0).reshape(TOK, D_MODEL)

    def heads(a, part):
        return a[:, :, part].transpose(2, 0, 1).reshape(1, 1, -1, HEADS, HD)

    def mem(a):
        return a.transpose(0, 3, 1, 2).reshape(DEPTH, 1, N_MEM, MEM_HEADS, HD)

    sample, prompt = slice(0, DEC), slice(DEC, TOK)
    out = {}
    for name, part in (("p", prompt), ("s", sample)):
        out[name] = (heads(got["k_o"][0], part), heads(got["v_o"][0], part),
                     got["lf_o"][:, part].T[None, None],
                     heads(got["k_o"][1], part), heads(got["v_o"][1], part))
    result = (y[prompt][None], y[sample][None], *out["p"], mem(got["mk_o"]), mem(got["mv_o"]), *out["s"])
    return tuple(np.ascontiguousarray(a) for a in result)
```

```python
from contextlib import ExitStack

import concourse.bass as bass
import concourse.mybir as mybir
import numpy as np
from concourse.alu_op_type import AluOpType as ALU

F32 = mybir.dt.float32
F32R = mybir.dt.float32r
BF16 = mybir.dt.bfloat16
ACT = mybir.ActivationFunctionType
AX = mybir.AxisListType.X

P = 128
D_MODEL = 1024
SEQ = 512
DEC = 64
PAST = 512
DEPTH = 2
HD = 64
HEADS = 12
N_MEM = 256
MEM_HEADS = 4
D_FF = 2816
EPS = 1e-6
SCALE = HD ** -0.5
BIG = 1e30

TOK = DEC + SEQ
HALF = TOK // 2
KT = D_MODEL // P
FT = D_FF // P
PAIRS = HEADS // 2
MEM_PAIRS = MEM_HEADS // 2
QT = SEQ // P
MB = N_MEM // P
KEYS_S = PAST + DEC
SLAB = KT * P
IN_TILES = 2 + 3 * PAIRS
OUT_TILES = KT
GU_TILES = 2 * FT
DOWN_CUTS = (8, 8, 6)
MKV_TILES = 4

MKV_SLABS = DEPTH * MKV_TILES
LAYER_TILES = IN_TILES + OUT_TILES + GU_TILES + KT
LAYER_SLABS = IN_TILES + OUT_TILES + GU_TILES + 3 * KT
ATTNS = MEM_PAIRS + PAIRS
UNITS = 2 * QT + 1

C_ID, C_MEAN, C_FOX, C_FOXS, C_SBN, C_SBNS, C_END = 0, 128, 256, 384, 448, 576, 640


SPARE = range(2, MKV_SLABS)
X_BESIDE = ((), (), (0, 1), (2,), (3,), (4,), (5,), (6, 7))


POOL_OUT = (0, 3)


def at_least(eng, sem, value):
    if not (isinstance(value, int) and value <= 0):
        eng.wait_ge(sem, value)


def build(nc, x_t, mem_t, w_mkv, w_in, w_f, w_out, w_gu, w_dn, gains, b_f, ck, cv, clf, cmk, cmv,
          consts, y_t, k_o, v_o, lf_o, mk_o, mv_o):
    ctx = ExitStack()
    region = ExitStack()

    def sb(name, shape, dt=F32, stack=ctx):
        return stack.enter_context(nc.sbuf_tensor(name, shape, dt))

    x = sb("x", [P, KT, TOK])
    xg_hi = sb("xg_hi", [P, KT, TOK], F32R)
    xg_lo = sb("xg_lo", [P, KT, TOK], F32R)
    w_raw = sb("w_raw", [P, 2, SLAB])
    w_hi = [sb(f"w_hi{i}", [P, SLAB], F32R) for i in range(2)]
    w_lo = [sb(f"w_lo{i}", [P, SLAB], F32R) for i in range(2)]
    cst = sb("cst", [P, C_END])
    gain = sb("gain", [P, 7 * KT])
    mk = sb("mk", [P, DEPTH, MEM_PAIRS, N_MEM])
    mv = sb("mv", [P, DEPTH, MEM_PAIRS, MB * P])
    rstd = sb("rstd", [P, TOK])
    sumsq = sb("sumsq", [P, TOK])
    work_a = sb("work_a", [P, 2, TOK])
    work_b = sb("work_b", [P, 2, TOK])
    work_c = sb("work_c", [P, 2, TOK])
    ident_b = sb("ident_b", [P, P], BF16)
    mask_b = sb("mask_b", [P, P + DEC], BF16)
    eps = sb("eps", [P, 1])
    least = sb("least", [P, 2])
    total = sb("total", [P, 2])
    inv = sb("inv", [P, 2])
    cq = sb("cq", [P, QT, HEADS])
    cq_s = sb("cq_s", [P, PAIRS])

    at = lambda name, shape, dt=F32: sb(name, shape, dt, region)
    qz = [at(f"qz{i}", [P, 2, TOK]) for i in range(2)]
    qs = [at(f"qs{i}", [P, 2 * DEC]) for i in range(2)]
    kb = [at(f"kb{i}", [P, PAST + TOK]) for i in range(2)]
    vcs = at("vcs", [P, 2, QT, P])
    vs = at("vs", [P, 2, QT, P])
    vc, v = ([t[:, i] for i in range(2)] for t in (vcs, vs))
    vn = [at(f"vn{i}", [P, P]) for i in range(2)]
    vf_z = at("vf_z", [P, DEC + TOK])
    vf = vf_z[:, DEC:]
    pt = at("pt", [P, QT, SEQ])
    pts = at("pts", [P, QT * P + P])
    gates = at("gates", [P, 2, 2, SEQ])
    ckb = [gates[:, i] for i in range(2)]
    ckbs = [at(f"ckbs{i}", [P, KEYS_S]) for i in range(2)]
    cum = at("cum", [HEADS, PAST + TOK])
    wf_raw = at("wf_raw", [P, KT * HEADS])
    wf_hi = at("wf_hi", [P, KT * HEADS], F32R)
    wf_lo = at("wf_lo", [P, KT * HEADS], F32R)
    bias_f = at("bias_f", [HEADS, 1])
    dup = sb("dup", [HEADS, P], F32, region)
    lf = sb("lf", [HEADS, PAST + TOK], F32, region)
    inner = ExitStack()
    o_hi = sb("o_hi", [P, KT, TOK], F32R, inner)
    o_lo = sb("o_lo", [P, KT, TOK], F32R, inner)
    inner.close()
    m_raw = sb("m_raw", [P, KT, N_MEM], F32, region)
    m_hi = [sb(f"m_hi{i}", [P, KT, N_MEM], F32R, region) for i in range(DEPTH)]
    m_lo = [sb("m_lo", [P, KT, N_MEM], F32R, region)[:, :, :],
            gates[:, :, :, :].bitcast(F32R).rearrange("p a b (k c) -> p (a b k) c", c=N_MEM)]
    region.close()
    f_hi = sb("f_hi", [P, FT, TOK], F32R)
    f_lo = sb("f_lo", [P, FT, TOK], F32R)
    spare = [tile[:, 0:SLAB] for tile in (qz[0][:, :, :].rearrange("p h c -> p (h c)"),
                                          qz[1][:, :, :].rearrange("p h c -> p (h c)"), kb[0], kb[1],
                                          vcs[:, :, :, :].rearrange("p i j c -> p (i j c)"),
                                          vs[:, :, :, :].rearrange("p i j c -> p (i j c)"))]
    mvt = pt[:, :, 0:N_MEM]
    m_sum = sumsq[:, 0:N_MEM]
    m_sq = pt[:, :, :].rearrange("p j (a c) -> p (j a) c", a=2)

    psum = lambda name, shape: ctx.enter_context(nc.psum_tensor(name, shape, F32))
    acc = psum("acc", [P, 2, 2, 512])
    score = psum("score", [P, 2, 512])
    turned = psum("turned", [P, 512])
    out_ps = psum("out_ps", [P, 512])

    sem = lambda name: ctx.enter_context(nc.semaphore(name))
    const_in = sem("const_in")
    gain_in = sem("gain_in")
    eps_set = sem("eps_set")
    masks_made = sem("masks_made")
    x_in = sem("x_in")
    mem_in = [sem(f"mem_in{i}") for i in range(2)]
    spare_in = [sem(f"spare_in{i}") for i in SPARE]
    w_arrived = [sem(f"w_arrived{i}") for i in range(2)]
    whi_made = sem("whi_made")
    wlo_made = sem("wlo_made")
    slab_done = sem("slab_done")
    acc_free = sem("acc_free")
    score_ready = sem("score_ready")
    score_free = sem("score_free")
    exp_in = sem("exp_in")
    exp_out = sem("exp_out")
    probs_ready = sem("probs_ready")
    soft_ready = sem("soft_ready")
    turned_ready = sem("turned_ready")
    turned_free = sem("turned_free")
    out_ready = sem("out_ready")
    out_hi = sem("out_hi")
    out_free = sem("out_free")
    qkv_ready = sem("qkv_ready")
    cache_in = [sem(f"cache_in{i}") for i in range(2)]
    cum_in = [sem(f"cum_in{i}") for i in range(2)]
    kv_stored = sem("kv_stored")
    mem_stored = sem("mem_stored")
    x_new = sem("x_new")
    xhi_made = sem("xhi_made")
    xlo_made = sem("xlo_made")
    sq_made = sem("sq_made")
    sq_added = sem("sq_added")
    rstd_made = sem("rstd_made")
    m_hi_made = sem("m_hi_made")
    m_lo_made = sem("m_lo_made")
    m_sq_made = sem("m_sq_made")
    m_sum_made = sem("m_sum_made")
    mem_kv = sem("mem_kv")
    wf_in = sem("wf_in")
    wf_hi_made = sem("wf_hi_made")
    wf_lo_made = sem("wf_lo_made")
    zeroed = sem("zeroed")
    gate_in = sem("gate_in")
    gate_soft = sem("gate_soft")
    cum_made = sem("cum_made")
    clf_in = sem("clf_in")
    lf_stored = sem("lf_stored")
    cum_out = sem("cum_out")
    gated = sem("gated")
    silu_made = sem("silu_made")
    prod_made = sem("prod_made")
    fhi_made = sem("fhi_made")
    flo_made = sem("flo_made")
    x_gained = sem("x_gained")
    y_made = sem("y_made")
    y_made_pool = sem("y_made_pool")
    y_stored = sem("y_stored")
    cum_dram = nc.dram_tensor("cum_dram", (HEADS, PAST + TOK), F32).ap()

    ident = cst[:, C_ID:C_ID + P]
    mean = cst[:, C_MEAN:C_MEAN + P]

    def raw(s, par, cols=SLAB):
        return spare[s - 2] if isinstance(s, int) and s in SPARE else w_raw[:, par, 0:cols]

    def halves(tile):
        return tile.rearrange("p (h c) -> p h c", h=2)

    def layer_slab(layer):
        return MKV_SLABS + layer * LAYER_SLABS

    def gu_slab(layer):
        return layer_slab(layer) + IN_TILES + OUT_TILES

    def layer_tile(layer):
        return MKV_SLABS + layer * LAYER_TILES

    LAYER_USE = [2, 8 + ATTNS * UNITS, 12 + 2 * ATTNS * UNITS]

    def attn_use(layer, a):
        return LAYER_USE[layer] + (4 if layer == 0 else 2) + a * UNITS

    MEM_ROUNDS = 2 * QT + 1
    PAIR_ROUNDS = 1 + 2 * QT + 2
    LAYER_ROUNDS = MEM_PAIRS * MEM_ROUNDS + PAIRS * PAIR_ROUNDS

    class Call:

        def __init__(self, layer, half, par, mem=False, tiles=(), spread=(0,) * UNITS, fill=0):
            self.layer, self.par, self.mem = layer, par, mem
            self.a = a = half * 2 + par
            self.last = isinstance(a, int) and a == ATTNS - 1
            self.stick = layer == 1 and not mem
            self.pair = None if mem else a - MEM_PAIRS
            self.o_tile = PAIRS + a if mem else a - MEM_PAIRS
            self.unit = (a + layer * ATTNS) * UNITS
            self.use = attn_use(layer, a)
            start = 2 * DEPTH + 1 + layer * LAYER_ROUNDS
            self.round = a * MEM_ROUNDS + start if mem else \
                a * PAIR_ROUNDS + (start + MEM_PAIRS * (MEM_ROUNDS - PAIR_ROUNDS))
            self.out = (a + layer * ATTNS) * 3
            self.qkv = layer * IN_TILES + a + 1 if mem else a * 3 + (layer * IN_TILES - 1)
            self.qk = self.qkv if mem else self.qkv - 1
            self.caches = (half + (layer * ATTNS // 2 + 1)) * 32
            self.cums = half * 64
            self.tiles = tiles
            self.slabs = [fill * 6 + (layer_slab(layer) + t) for t, _ in tiles]
            self.nums = [fill * 6 + (layer_tile(layer) + t) for t, _ in tiles]
            self.spread = spread
            beside = [u for u, n in enumerate(spread) for _ in range(n)]
            self.per = len(beside) // len(tiles) if tiles else 0
            self.starts = [beside[self.per * n] for n in range(len(tiles))] if beside else []
            self.ends = [beside[self.per * n + self.per - 1] for n in range(len(tiles))] if beside else []

        def sample_out(self):
            return score[:, 0, 0:P] if self.last else out_ps[:, 0:P]

        def buf(self, u):
            return (self.par + u) % 2

        def used(self, u):
            return self.use + (u + 1)

        def parts(self, u):
            w = self.width(u)
            if w > 512:
                return [(score[:, self.buf(u), 0:PAST], slice(0, PAST)), (out_ps[:, 0:DEC], slice(PAST, w))]
            return [(score[:, self.buf(u), 0:w], slice(0, w))]

        def width(self, u):
            if u == 2 * QT:
                return N_MEM if self.mem else KEYS_S
            return N_MEM if self.mem else (u % QT + 1) * P

        def turned_round(self, u):
            return self.round + (u if self.mem else u + 1)

    def calls(eng, layer, call):
        def pair(half, par, t, fill=0):
            return Call(layer, half, par, False, [(t + c, "qkv"[c]) for c in range(3)],
                        (2, 2, 4, 3, 3, 2, 3, 3, 2), fill)

        mem0 = Call(layer, 0, 0, True, [(2, "k")], (1,) * 8 + (0,))
        mem1 = Call(layer, 0, 1, True, [(3, "q"), (4, "v")], (2,) * 7 + (1, 1))
        pair0 = pair(1, 0, 5)
        last = Call(layer, ATTNS // 2 - 1, 1, False, [(IN_TILES, "o"), (IN_TILES + 1, "o")],
                    (0, 1, 2, 1, 1, 0, 0, 1, 1) + (1,) * 7)
        call(mem0, None, mem1)
        call(mem1, mem0, pair0)
        call(pair0, mem1, pair(1, 1, 8))
        with eng.Fori(0, (PAIRS - 2) // 2) as i:
            odd, even = pair(i + 1, 1, 8, i), pair(i + 2, 0, 11, i)
            call(odd, pair(i + 1, 0, 5, i), even)
            call(even, odd, pair(i + 2, 1, 14, i))
        call(last, pair(ATTNS // 2 - 1, 0, 5), None)

    block = ctx.enter_context(nc.Block())

    @block.sync
    def _(sp):
        def slab(s, par, src, cols=SLAB):
            if isinstance(s, int) and s in SPARE:
                sp.dma_start(raw(s, par), src).then_inc(spare_in[s - 2], 16)
                return
            at_least(sp, wlo_made, s - 7 if isinstance(s, int) and s < 10 else s - 1)
            sp.dma_start(w_raw[:, par, 0:cols], src).then_inc(w_arrived[par], 16)

        def cache(layer, half, par, mem):
            c = Call(layer, half, par, mem)
            at_least(sp, out_ready, 0 if layer == 0 and mem else c.out - 3)
            if mem:
                sp.dma_start(kb[par][:, 0:N_MEM], cmk[layer, par]).then_inc(cache_in[par], 16)
                sp.dma_start(vc[par][:, 0:MB, :], cmv[layer, par].rearrange("p (j c) -> p j c", j=MB)) \
                    .then_inc(cache_in[par], 16)
                return
            sp.dma_start(kb[par][:, 0:PAST], ck[layer, bass.ds(c.pair, 1)].rearrange("a p c -> (a p) c")) \
                .then_inc(cache_in[par], 16)
            sp.dma_start(vc[par][:, :, :], cv[layer, bass.ds(c.pair, 1)].rearrange("a p (j c) -> (a p) j c", j=QT)) \
                .then_inc(cache_in[par], 16)
            if layer == 0:
                sp.wait_ge(cum_out, 16)
                for hd in range(2):
                    row = cum_dram[bass.ds(c.pair * 2 + hd, 1), :]
                    sp.dma_start(ckb[par][:, hd, :], row[:, KEYS_S:].to_broadcast([P, SEQ])) \
                        .then_inc(cum_in[par], 16)
                    sp.dma_start(ckbs[par][hd * HD:(hd + 1) * HD, :],
                                 row[:, 0:KEYS_S].to_broadcast([HD, KEYS_S])).then_inc(cum_in[par], 16)

        slab(0, 0, w_mkv[0, 0])
        sp.dma_start(gain[:, :], gains).then_inc(gain_in, 16)
        for n in range(2):
            tiles = slice(n * KT // 2, (n + 1) * KT // 2)
            sp.dma_start(m_raw[:, tiles, :], mem_t[:, tiles, :]).then_inc(mem_in[n], 16)
        slab(1, 1, w_mkv[0, 1])
        sp.dma_start(cst[:, :], consts).then_inc(const_in, 16)
        for s in range(2, 4):
            slab(s, s % 2, w_mkv[0, s])
        sp.dma_start(x[:, :, :], x_t).then_inc(x_in, 16)
        for s in range(4, MKV_SLABS):
            slab(s, s % 2, w_mkv[1, s % MKV_TILES])
        sp.dma_start(wf_raw[:, :], w_f).then_inc(wf_in, 16)
        sp.dma_start(bias_f[:, :], b_f).then_inc(wf_in, 16)
        sp.dma_start(lf[:, 0:PAST], clf).then_inc(clf_in, 16)
        for layer in range(DEPTH):
            s0 = layer_slab(layer)
            for t in range(2):
                slab(s0 + t, t, w_in[layer, t])
            if layer:
                sp.wait_ge(slab_done, s0)
            else:
                sp.wait_ge(wlo_made, MKV_SLABS)
            cache(layer, 0, 0, True)
            cache(layer, 0, 1, True)
            for t in range(2, 8):
                slab(s0 + t, t % 2, w_in[layer, t])
                if t in (5, 6):
                    cache(layer, 1, t - 5, False)
            with sp.Fori(0, (PAIRS - 2) // 2) as i:
                for par in range(2):
                    for c in range(3):
                        t = 8 + 3 * par + c
                        slab(i * 6 + (s0 + t), t % 2,
                             w_in[layer, bass.ds(i * 6 + t, 1)].rearrange("a p c -> (a p) c"))
                        if c == 1:
                            cache(layer, i + 2, par, False)
            for first, src, count in ((s0 + IN_TILES, w_out, OUT_TILES), (gu_slab(layer), w_gu, GU_TILES)):
                with sp.Fori(0, count // 2) as i:
                    for j in range(2):
                        slab(i * 2 + (first + j), j,
                             src[layer, bass.ds(i * 2 + j, 1)].rearrange("a p c -> (a p) c"))
            with sp.Fori(0, KT // 2) as i:
                for n in range(6):
                    m, c = divmod(n, 3)
                    cols = DOWN_CUTS[c] * P
                    src = w_dn[layer, bass.ds(i * 2 + m, 1)].rearrange("a p c -> (a p) c")
                    slab(i * 6 + (gu_slab(layer) + GU_TILES + n), n % 2,
                         src[:, c * SLAB:c * SLAB + cols], cols)
        dve_out = 0
        for k in (1, 2, 0, 4, 5, 3, 6, 7):
            if k in POOL_OUT:
                sp.wait_ge(y_made_pool, POOL_OUT.index(k) + 1)
            else:
                dve_out += 1
                sp.wait_ge(y_made, dve_out)
            sp.dma_start(y_t[:, k, :], x[:, k, :]).then_inc(y_stored, 16)
        sp.wait_ge(y_stored, 16 * KT)
        sp.wait_ge(kv_stored, 32 * DEPTH * PAIRS)
        sp.wait_ge(mem_stored, 16 * MKV_SLABS)
        sp.wait_ge(lf_stored, 16)

    @block.gpsimd
    def _(pool):
        def low(s, par, cols=SLAB):
            pool.wait_ge(whi_made, s + 1)
            pool.tensor_tensor(w_lo[par][:, 0:cols], raw(s, par, cols),
                               w_hi[par][:, 0:cols].bitcast(F32), ALU.subtract).then_inc(wlo_made, 1)

        def add_square(norm, m):
            if m:
                if m > 1:
                    pool.wait_ge(sq_added, norm * (KT - 1) + m - 1)
                pool.wait_ge(sq_made, norm * KT + m + 1)
                pool.tensor_tensor(sumsq[:, :], sumsq[:, :], work_c[:, m % 2, :], ALU.add) \
                    .then_inc(sq_added, 1)

        def zero_rows(layer):
            tiles = [vf_z[:, 0:DEC]]
            for par in range(2):
                tiles += [qz[par][HD:P, 0, :], qz[par][0:HD, 1, :], qs[par][HD:P, 0:DEC], qs[par][0:HD, DEC:]]
            for n, tile in enumerate(tiles):
                pool.memset(tile, 0.0).then_inc(zeroed, 1)
                pool.wait_ge(zeroed, len(tiles) * layer + n + 1)

        for n in range(2):
            tiles = slice(n * KT // 2, (n + 1) * KT // 2)
            pool.wait_ge(mem_in[n], 16)
            pool.tensor_tensor(m_sq[:, tiles, :], m_raw[:, tiles, :], m_raw[:, tiles, :], ALU.mult) \
                .then_inc(m_sq_made, 1)
        for m in range(KT - 3):
            add_square(0, m)
        pool.wait_ge(wlo_made, MKV_SLABS)
        low(MKV_SLABS, 0)
        pool.wait_ge(wf_hi_made, 1)
        pool.tensor_tensor(wf_lo[:, :], wf_raw[:, :], wf_hi[:, :].bitcast(F32), ALU.subtract) \
            .then_inc(wf_lo_made, 1)
        for m in range(KT - 3, KT):
            add_square(0, m)
        for layer in range(DEPTH):
            s0 = layer_slab(layer)
            low(s0 + 1, 1)
            if layer:
                pool.wait_ge(slab_done, s0)
            zero_rows(layer)
            with pool.Fori(1, IN_TILES // 2) as i:
                for j in range(2):
                    low(i * 2 + (s0 + j), j)
            for m in range(OUT_TILES):
                if m == 2:
                    pool.wait_ge(wlo_made, s0 + IN_TILES + 3)
                else:
                    low(s0 + IN_TILES + m, m % 2)
                if m:
                    add_square(2 * layer + 1, m - 1)
            low(gu_slab(layer), 0)
            add_square(2 * layer + 1, KT - 1)
            low(gu_slab(layer) + 1, 1)
            with pool.Fori(1, GU_TILES // 2) as i:
                for j in range(2):
                    low(i * 2 + (gu_slab(layer) + j), j)
            for m in range(KT):
                for c, cut in enumerate(DOWN_CUTS):
                    low(gu_slab(layer) + GU_TILES + 3 * m + c, (3 * m + c) % 2, cut * P)
                if m:
                    add_square(2 * layer + 2, m - 1)
            if layer < DEPTH - 1:
                low(layer_slab(layer + 1), 0)
            if layer < DEPTH - 1:
                add_square(2 * layer + 2, KT - 1)
        for k in POOL_OUT:
            pool.wait_ge(rstd_made, 2 * DEPTH + 2)
            pool.wait_ge(x_gained, POOL_OUT.index(k) + 1)
            pool.tensor_tensor(x[:, k, :], x[:, k, :], rstd[:, :], ALU.mult).then_inc(y_made_pool, 1)

    @block.tensor
    def _(pe):
        def passes(par, k, hi, lo, tpar, first, last):
            width = hi.shape[-1]
            cuts = ((0, HALF), (HALF, TOK)) if width == TOK else ((0, width),)
            parts = ((w_hi, hi), (w_hi, lo), (w_lo, hi))
            for n, (w, a) in enumerate(parts):
                for h, (c0, c1) in enumerate(cuts):
                    mm = pe.matmul(acc[:, tpar, h, 0:c1 - c0], w[par][:, k * P:(k + 1) * P], a[:, c0:c1],
                                   start=first and n == 0, stop=last and n == 2)
            return mm

        def begin(s, t):
            pe.wait_ge(wlo_made, s + 1)
            at_least(pe, acc_free, t - 1)

        def product(s, t, par, tpar, hi, lo, kts=KT, k0=0, first=True, last=True, before=None):
            begin(s, t)
            for k in range(kts):
                if before is not None:
                    before(k0 + k)
                mm = passes(par, k, hi[:, k0 + k, :], lo[:, k0 + k, :], tpar,
                            first and k == 0, last and k == kts - 1)
            mm.then_inc(slab_done, 1)

        def norm_sum(norm, use):
            pe.wait_ge(sq_added, (KT - 1) * (norm + 1))
            pe.wait_ge(score_free, use)
            for h in range(2):
                pe.matmul(score[:, h, 0:HALF], mean, sumsq[:, h * HALF:(h + 1) * HALF],
                          start=True, stop=True).then_inc(score_ready, 1)

        def turn_mem(s):
            n = 2 * (s // MKV_TILES) + s % 2
            pe.wait_ge(mem_kv, s + 1)
            at_least(pe, turned_free, n)
            for j in range(MB):
                mm = pe.transpose(turned[:, j * P:(j + 1) * P], mvt[:, n, j * P:(j + 1) * P], ident)
            mm.then_inc(turned_ready, 1)

        for s in range(MKV_SLABS):
            layer = s // MKV_TILES
            product(s, s, s % 2, s % 2, m_hi[layer], m_lo[layer],
                    before=lambda k: pe.wait_ge(m_lo_made, KT * layer + k + 1))
            if s == 1:
                pe.wait_ge(const_in, 16)
                pe.wait_ge(m_sum_made, 1)
                for h in range(2):
                    pe.matmul(score[:, h, 0:P], mean, m_sum[:, h * P:(h + 1) * P],
                              start=True, stop=True).then_inc(score_ready, 1)
            if s and (s - 1) % MKV_TILES >= 2:
                turn_mem(s - 1)

        def scores(c, u):
            if u == 0:
                pe.wait_ge(qkv_ready, c.qk)
            sample = u == 2 * QT
            hd, i = divmod(u, QT)
            if sample:
                pe.wait_ge(cache_in[c.par], c.caches)
                query = qs[c.par][:, :]
                if not c.mem:
                    pe.wait_ge(out_free, c.out + 1)
                keys, own = kb[c.par], 0
            else:
                query = qz[c.par][:, hd, DEC + i * P:DEC + (i + 1) * P]
                keys, own = (mk[:, c.layer, c.par, :], 0) if c.mem else (kb[c.par], KEYS_S)
            pe.wait_ge(score_free, c.use + (u - 1))
            parts = c.parts(u)
            for n, (out, cols) in enumerate(parts):
                masked = c.stick and n == len(parts) - 1
                mm = pe.matmul(out, query, keys[:, own + cols.start:own + cols.stop],
                               start=True, stop=not masked)
            if c.stick:
                mask = mask_b[:, P:] if sample else mask_b[:, 0:P]
                out, width = parts[-1][0], mask.shape[-1]
                mm = pe.matmul(out[:, out.shape[-1] - width:], ident_b[:, :], mask, start=False, stop=True)
            mm.then_inc(score_ready, 1)

        def turn_blocks(n, tile, blocks, beside=None):
            pe.wait_ge(turned_free, n)
            for j in range(blocks):
                mm = pe.transpose(turned[:, j * P:(j + 1) * P], tile[:, j * P:(j + 1) * P], ident)
            if beside is not None:
                mm = pe.transpose(turned[:, blocks * P:(blocks + 1) * P], beside, ident)
            mm.then_inc(turned_ready, 1)

        def turn(c, u):
            pe.wait_ge(probs_ready, c.unit + (u + 1))
            turn_blocks(c.turned_round(u), work_b[:, c.buf(u), :], c.width(u) // P,
                        vf_z[:, 0:P] if u == 0 and not c.mem else None)

        def turn_rest(c):
            if not c.mem:
                turn_blocks(c.turned_round(2 * QT) + 1,
                            work_b[:, c.buf(2 * QT), KEYS_S - P:KEYS_S], 1)

        def values(c, hd):
            pe.wait_ge(turned_free, c.turned_round(QT * (hd + 1) - 1) + 1)
            if hd and not c.mem:
                pe.wait_ge(score_free, c.used(2 * QT))
            at_least(pe, out_free, c.out + hd)
            count = MB if c.mem else QT
            for j in range(count):
                c0 = 0 if c.mem else j * P
                val = mv[:, c.layer, c.par, j * P:(j + 1) * P] if c.mem else v[c.par][:, j, :]
                mm = pe.matmul(out_ps[:, c0:SEQ], val, pt[:, j, c0:SEQ], start=(j == 0),
                               stop=(j == count - 1), skip_group_check=True)
            mm.then_inc(out_ready, 1)

        def values_sample(c):
            pe.wait_ge(turned_free, c.turned_round(2 * QT) + (1 if c.mem else 2))
            if not c.last:
                pe.wait_ge(out_free, c.out + 2)
            count = MB if c.mem else QT
            for j in range(count):
                mm = pe.matmul(c.sample_out(), vc[c.par][:, j, :], pts[:, j * P:(j + 1) * P],
                               start=(j == 0), stop=(c.mem and j == count - 1))
            if not c.mem:
                mm = pe.matmul(c.sample_out(), vn[c.par][:, :], pts[:, QT * P:],
                               start=False, stop=True)
            mm.then_inc(out_ready, 1)

        def attention(c, prev, nxt):
            done = [0]

            def fill(pieces):
                for g in range(done[0], done[0] + pieces):
                    n, k = divmod(g, c.per)
                    slot = c.tiles[n][0] % 2
                    if k == 0:
                        begin(c.slabs[n], c.nums[n])
                    if c.tiles[n][1] == "o":
                        row = (PAIRS, PAIRS + 1, 0, 1, 2, 3, 4)[k]
                        if row == 4:
                            pe.wait_ge(out_free, c.out)
                        passes(slot, row, o_hi[:, row, :], o_lo[:, row, :], slot, k == 0, False)
                    else:
                        mm = passes(slot, k, xg_hi[:, k, :], xg_lo[:, k, :], slot, k == 0, k == KT - 1)
                        if k == KT - 1:
                            mm.then_inc(slab_done, 1)
                done[0] += pieces

            if prev is None:
                scores(c, 0)
                scores(c, 1)
            for u in range(UNITS):
                pieces = c.spread[u]
                half = pieces // 2
                fill(pieces - half)
                if u == 0 and prev is not None:
                    turn(prev, 2 * QT)
                    values(prev, 1)
                    turn_rest(prev)
                if u == 1 and not c.mem:
                    pe.wait_ge(qkv_ready, c.qkv)
                    turn_blocks(c.round, vf[:, DEC:], QT)
                if u == 1 and prev is not None:
                    values_sample(prev)
                if u == QT + 1:
                    values(c, 0)
                fill(half)
                if u:
                    turn(c, u - 1)
                if u + 2 < UNITS:
                    scores(c, u + 2)
                elif nxt is not None:
                    scores(nxt, u + 2 - UNITS)
            if nxt is None:
                fill(2)
                turn(c, 2 * QT)
                fill(1)
                values(c, 1)
                turn_rest(c)
                fill(1)
                values_sample(c)
                fill(1)
                pe.wait_ge(out_free, c.out + 3)
                for n in range(2):
                    passes(n, PAIRS - 1, o_hi[:, PAIRS - 1, :], o_lo[:, PAIRS - 1, :], n, False, True) \
                        .then_inc(slab_done, 1)
                    if n == 0:
                        fill(2)

        for layer in range(DEPTH):
            s0, t0 = layer_slab(layer), layer_tile(layer)
            product(s0, t0, 0, 0, xg_hi, xg_lo,
                    before=lambda k: pe.wait_ge(xlo_made, KT * 2 * layer + k + 1))
            if layer == 0:
                turn_mem(MKV_SLABS - 1)
            norm_sum(2 * layer, LAYER_USE[layer])
            if layer == 0:
                pe.wait_ge(wf_lo_made, 1)
                pe.wait_ge(score_free, LAYER_USE[layer] + 2)
                for h in range(2):
                    for k in range(KT):
                        parts = ((wf_hi, xg_hi), (wf_hi, xg_lo), (wf_lo, xg_hi))
                        for n, (w, a) in enumerate(parts):
                            mm = pe.matmul(score[0:HEADS, h, 0:HALF], w[:, k * HEADS:(k + 1) * HEADS],
                                           a[:, k, h * HALF:(h + 1) * HALF],
                                           start=(k == 0 and n == 0), stop=(k == KT - 1 and n == 2))
                    mm.then_inc(score_ready, 1)
            product(s0 + 1, t0 + 1, 1, 1, xg_hi, xg_lo)
            if layer == 0:
                pe.wait_ge(cum_made, 1)
                pe.wait_ge(turned_free, 2 * DEPTH)
                for i in range(QT):
                    pe.transpose(turned[:, i * HEADS:(i + 1) * HEADS],
                                 cum[:, KEYS_S + i * P:KEYS_S + (i + 1) * P], ident[0:HEADS, 0:HEADS])
                pe.transpose(turned[:, QT * HEADS:(QT + 1) * HEADS], dup[:, :],
                             ident[0:HEADS, 0:HEADS]).then_inc(turned_ready, 1)
            pe.wait_ge(zeroed, 9 * (layer + 1))
            pe.wait_ge(masks_made, 1)
            calls(pe, layer, attention)

            so, to = s0 + IN_TILES, t0 + IN_TILES
            with pe.Fori(1, OUT_TILES // 2) as i:
                for j in range(2):
                    product(i * 2 + (so + j), i * 2 + (to + j), j, j, o_hi, o_lo)

            sg, tg = so + OUT_TILES, to + OUT_TILES
            product(sg, tg, 0, 0, xg_hi, xg_lo,
                    before=lambda k: pe.wait_ge(xlo_made, KT * (2 * layer + 1) + k + 1))
            norm_sum(2 * layer + 1, attn_use(layer, ATTNS))
            for j in range(1, 4):
                product(sg + j, tg + j, j % 2, j % 2, xg_hi, xg_lo)
            with pe.Fori(1, GU_TILES // 4) as i:
                for j in range(4):
                    product(i * 4 + (sg + j), i * 4 + (tg + j), j % 2, j % 2, xg_hi, xg_lo)

            sd, td = sg + GU_TILES, tg + GU_TILES

            def down(i, m, before=None):
                k0 = 0
                for n, cut in enumerate(DOWN_CUTS):
                    product(i * 6 + (sd + 3 * m + n), i * 2 + (td + m), (3 * m + n) % 2, m, f_hi, f_lo, cut, k0,
                            n == 0, n == len(DOWN_CUTS) - 1, before)
                    k0 += cut

            down(0, 0, lambda k: pe.wait_ge(flo_made, layer * FT + k + 1))
            down(0, 1)
            with pe.Fori(1, KT // 2) as i:
                down(i, 0)
                down(i, 1)
        pe.wait_ge(sq_added, (KT - 1) * (2 * DEPTH + 1) - 1)
        pe.wait_ge(sq_made, KT * (2 * DEPTH + 1))
        pe.wait_ge(score_free, LAYER_USE[DEPTH])
        for h in range(2):
            cols = slice(h * HALF, (h + 1) * HALF)
            pe.matmul(score[:, h, 0:HALF], mean, sumsq[:, cols], start=True, stop=False)
            pe.matmul(score[:, h, 0:HALF], mean, work_c[:, (KT - 1) % 2, cols],
                      start=False, stop=True).then_inc(score_ready, 1)

    @block.scalar
    def _(act):
        def high(s, par, cols=SLAB):
            if isinstance(s, int) and s in SPARE:
                act.wait_ge(spare_in[s - 2], 16)
            else:
                act.wait_ge(w_arrived[par], 16 if isinstance(s, int) and s < 2 else (s - par) * 8 - 32)
            at_least(act, slab_done, s - 1)
            act.activation(w_hi[par][:, 0:cols], raw(s, par, cols), ACT.Copy).then_inc(whi_made, 1)

        def factor(use, width=TOK):
            act.wait_ge(score_ready, use + 2)
            out = rstd[:, 0:width]
            act.activation(halves(out), score[:, :, 0:width // 2], ACT.Ln, bias=eps[:, :]).then_inc(score_free, 2)
            act.drain()
            act.activation(out, out, ACT.Exp, scale=-0.5).then_inc(rstd_made, 1)

        def split_x(norm, m, g):
            if norm:
                act.wait_ge(x_new, KT * (norm - 1) + m + 1)
            if g is not None:
                act.activation(xg_hi[:, m, :], x[:, m, :], ACT.Copy,
                               scale=gain[:, g * KT + m:g * KT + m + 1]).then_inc(xhi_made, 1)
            if m > 2:
                act.wait_ge(sq_added, (KT - 1) * norm + m - 2)
            square = sumsq[:, :] if m == 0 else work_c[:, m % 2, :]
            act.activation(square, x[:, m, :], ACT.Square).then_inc(sq_made, 1)

        def split_mem(layer):
            for k in range(KT):
                c = (2 + layer) * KT + k
                if layer == 0 and k % (KT // 2) == 0:
                    act.wait_ge(mem_in[k // (KT // 2)], 16)
                act.activation(m_hi[layer][:, k, :], m_raw[:, k, :], ACT.Copy, scale=gain[:, c:c + 1]) \
                    .then_inc(m_hi_made, 1)

        act.preload_act_table_set("natural_log_exp_and_others")
        high(0, 0)
        act.wait_ge(gain_in, 16)
        split_mem(0)
        high(1, 1)
        high(2, 0)
        act.wait_ge(eps_set, 1)
        factor(0, N_MEM)

        def copy_mem(s):
            n = 2 * (s // MKV_TILES) + s % 2
            act.wait_ge(turned_ready, n + 1)
            act.activation(mv[:, s // MKV_TILES, s % 2, :], turned[:, 0:N_MEM], ACT.Copy) \
                .then_inc(turned_free, 1)

        for s in range(MKV_SLABS):
            layer, c = divmod(s, MKV_TILES)
            if s:
                high(s + 2, s % 2)
            act.wait_ge(mem_kv, s + 1)
            source = mk[:, layer, c, :] if c < 2 else mvt[:, 2 * layer + c - 2, :]
            act.dma_start((mk_o if c < 2 else mv_o)[layer, c % 2], source).then_inc(mem_stored, 16)
            if s and (s - 1) % MKV_TILES >= 2:
                copy_mem(s - 1)
            if s == 1:
                split_mem(1)
                act.wait_ge(x_in, 16)
            if s == 6:
                act.wait_ge(wf_in, 32)
                act.activation(wf_hi[:, :], wf_raw[:, :], ACT.Copy).then_inc(wf_hi_made, 1)
            for m in X_BESIDE[s]:
                split_x(0, m, 0)
        act.wait_ge(const_in, 16)
        act.activation(ident_b[:, :], ident, ACT.Copy)
        act.activation(mask_b[:, :], cst[:, C_SBN:C_END], ACT.Copy).then_inc(masks_made, 1)
        copy_mem(MKV_SLABS - 1)

        def softplus(c, u):
            b, w = c.buf(u), c.width(u)
            act.wait_ge(score_ready, c.used(u))
            for z, cols in c.parts(u):
                act.activation(work_c[:, b, cols], z, ACT.Abs)
            act.drain()
            flat = work_c[:, b, 0:w]
            act.activation(flat, flat, ACT.Exp, scale=-1.0)
            act.drain()
            act.activation(flat, flat, ACT.Ln, bias=1.0).then_inc(soft_ready, 1)

        def exponential(c, u):
            b, w = c.buf(u), c.width(u)
            act.wait_ge(exp_in, c.unit + (u + 1))
            if c.stick:
                act.activation(work_b[:, b, 0:w], work_a[:, b, 0:w], ACT.Exp).then_inc(probs_ready, 1)
            else:
                act.activation(work_b[:, b, 0:w], work_a[:, b, 0:w], ACT.Exp, bias=least[:, b:b + 1],
                               scale=-1.0, accum_out=total[:, b:b + 1]).then_inc(exp_out, 1)

        def copy_round(n, out, src):
            act.wait_ge(turned_ready, n + 1)
            act.activation(out, src, ACT.Copy).then_inc(turned_free, 1)

        def copy_turned(c, u):
            n = c.width(u) // P
            if u < 2 * QT:
                i = u % QT
                if u == 0 and not c.mem:
                    act.wait_ge(turned_ready, c.turned_round(u) + 1)
                    act.activation(vn[c.par][:, :], turned[:, P:2 * P], ACT.Copy)
                copy_round(c.turned_round(u), pt[:, 0:n, i * P:(i + 1) * P],
                           turned[:, 0:n * P].rearrange("p (j q) -> p j q", j=n))
                return
            copy_round(c.turned_round(u), pts[:, 0:n * P], turned[:, 0:n * P])
            if not c.mem:
                copy_round(c.turned_round(u) + 1, pts[:, QT * P:], turned[:, 0:P])

        def out_high(c, n):
            act.wait_ge(out_ready, c.out + (n + 1))
            tile = bass.ds(c.o_tile, 1)
            for hd in range(2):
                if n != 1 - hd:
                    rows = slice(hd * HD, (hd + 1) * HD)
                    cols = slice(0, DEC) if n == 2 else slice(DEC, TOK)
                    src = c.sample_out()[rows, hd * DEC:(hd + 1) * DEC] if n == 2 else out_ps[rows, :]
                    last = act.activation(o_hi[rows, tile, cols],
                                          src.rearrange("p (a c) -> p a c", a=1), ACT.Copy)
            last.then_inc(out_hi, 1)

        def attention(c, prev, nxt):
            if prev is None and c.stick:
                softplus(c, 0)
            for u in range(UNITS):
                if c.stick and u + 1 < UNITS:
                    softplus(c, u + 1)
                if u + 1 == UNITS and nxt is not None and nxt.stick:
                    softplus(nxt, 0)
                exponential(c, u)
                if u == 0 and prev is not None:
                    copy_turned(prev, 2 * QT)
                    out_high(prev, 1)
                if u == 1 and not c.mem:
                    copy_round(c.round, v[c.par][:, :, :], turned[:, :].rearrange("p (j c) -> p j c", j=QT))
                if u:
                    copy_turned(c, u - 1)
                if u == 1 and prev is not None:
                    out_high(prev, 2)
                if u == QT + 1:
                    out_high(c, 0)
                if u in c.starts:
                    n = c.starts.index(u)
                    if c.tiles[n][0] != IN_TILES + 1:
                        high(c.slabs[n] + 1, (c.tiles[n][0] + 1) % 2)
                if u == 1 and not c.mem:
                    act.wait_ge(qkv_ready, c.qkv)
                    pair = bass.ds(c.pair, 1)
                    act.dma_start(k_o[c.layer, pair].rearrange("a p c -> (a p) c"), kb[c.par][:, PAST:]) \
                        .then_inc(kv_stored, 16)
                    act.dma_start(v_o[c.layer, pair].rearrange("a p c -> (a p) c"), vf[:, :]) \
                        .then_inc(kv_stored, 16)
            if nxt is None:
                copy_turned(c, 2 * QT)
                out_high(c, 1)
                out_high(c, 2)

        for layer in range(DEPTH):
            s0 = layer_slab(layer)
            high(s0 + 2, 0)
            factor(LAYER_USE[layer])
            if layer == 0:
                act.wait_ge(gate_in, 1)
                soft = work_b[0:HEADS, 0, :]
                act.activation(soft, work_a[0:HEADS, 0, :], ACT.Abs)
                act.drain()
                act.activation(soft, soft, ACT.Exp, scale=-1.0)
                act.drain()
                act.activation(soft, soft, ACT.Ln, bias=1.0).then_inc(gate_soft, 1)
                act.wait_ge(cum_made, 1)
                act.dma_start(cum_dram, cum[:, :]).then_inc(cum_out, 16)
                act.dma_start(lf_o, lf[:, PAST:]).then_inc(lf_stored, 16)
            if layer == 0:
                act.wait_ge(turned_ready, 2 * DEPTH + 1)
                act.activation(cq[:, :, :], turned[:, 0:QT * HEADS].rearrange("p (i h) -> p i h", i=QT),
                               ACT.Copy)
                for hd in range(2):
                    rows = slice(hd * HD, (hd + 1) * HD)
                    last = act.activation(cq_s[rows, :],
                                          turned[rows, QT * HEADS + hd:(QT + 1) * HEADS:2], ACT.Copy)
                last.then_inc(turned_free, 1)
                act.wait_ge(mem_stored, 16 * MKV_SLABS)
            calls(act, layer, attention)
            for m in range(OUT_TILES):
                if m < OUT_TILES - 1:
                    high(s0 + IN_TILES + m + 2, m % 2)
                split_x(2 * layer + 1, m, 4 + layer)
            high(s0 + IN_TILES + OUT_TILES + 1, 1)
            sg = gu_slab(layer)

            def gate_up(j, first=False):
                n = j + (layer * FT + 1)
                high(j * 2 + (sg + 2), 0)
                if first:
                    factor(attn_use(layer, ATTNS))
                act.wait_ge(gated, n)
                act.activation(work_b[:, 0, :], work_a[:, 0, :], ACT.Silu).then_inc(silu_made, 1)
                high(j * 2 + (sg + 3), 1)
                act.wait_ge(prod_made, n)
                act.activation(f_hi[:, bass.ds(j, 1), :], work_c[:, 0:1, :], ACT.Copy).then_inc(fhi_made, 1)

            act.wait_ge(kv_stored, 32 * PAIRS * (layer + 1))
            gate_up(0, True)
            with act.Fori(1, FT) as j:
                gate_up(j)
            act.preload_act_table_set("natural_log_exp_and_others")
            sd = sg + GU_TILES
            for m in range(KT):
                for s in range(3 * m + 2, 3 * m + 5):
                    if s < 3 * KT or (layer < DEPTH - 1 and s == 3 * KT):
                        high(sd + s, s % 2, (DOWN_CUTS[s % 3] if s < 3 * KT else KT) * P)
                split_x(2 * layer + 2, m, 1 if layer == 0 else None)
                if layer == DEPTH - 1 and m in POOL_OUT:
                    act.drain()
                    act.activation(x[:, m, :], x[:, m, :], ACT.Copy,
                                   scale=gain[:, 6 * KT + m:6 * KT + m + 1]).then_inc(x_gained, 1)
            if layer < DEPTH - 1:
                high(layer_slab(layer + 1) + 1, 1)
        factor(LAYER_USE[DEPTH])

    @block.vector
    def _(dve):
        def x_low(norm, m, g):
            dve.wait_ge(xhi_made, KT * norm + m + 1)
            dve.scalar_tensor_tensor(out=xg_lo[:, m, :], in0=x[:, m, :],
                                     scalar=gain[:, g * KT + m:g * KT + m + 1],
                                     in1=xg_hi[:, m, :].bitcast(F32), op0=ALU.mult,
                                     op1=ALU.subtract).then_inc(xlo_made, 1)

        def mem_low(layer, ks):
            for k in ks:
                dve.wait_ge(m_hi_made, layer * KT + k + 1)
                c = (2 + layer) * KT + k
                dve.scalar_tensor_tensor(out=m_lo[layer][:, k, :], in0=m_raw[:, k, :], scalar=gain[:, c:c + 1],
                                         in1=m_hi[layer][:, k, :].bitcast(F32), op0=ALU.mult,
                                         op1=ALU.subtract).then_inc(m_lo_made, 1)

        dve.memset(eps[:, :], EPS).then_inc(eps_set, 1)

        def low(s):
            dve.wait_ge(whi_made, s + 1)
            dve.tensor_tensor(w_lo[s % 2][:, :], raw(s, s % 2), w_hi[s % 2][:, :].bitcast(F32),
                              ALU.subtract).then_inc(wlo_made, 1)

        low(0)
        dve.wait_ge(gain_in, 16)
        mem_low(0, range(KT))
        low(1)
        dve.wait_ge(m_sq_made, 2)
        dve.tensor_reduce(m_sum, m_sq.rearrange("p k c -> p c k"), AX, ALU.add).then_inc(m_sum_made, 1)
        low(2)
        dve.wait_ge(rstd_made, 1)
        for s in range(MKV_SLABS):
            layer, c = divmod(s, MKV_TILES)
            dve.wait_ge(slab_done, s + 1)
            out = mk[:, layer, c, :] if c < 2 else mvt[:, 2 * layer + c - 2, :]
            dve.tensor_tensor(out, acc[:, s % 2, 0, 0:N_MEM], rstd[:, 0:N_MEM], ALU.mult) \
                .then_inc(mem_kv, 1)
            dve.drain()
            dve.sem_inc(acc_free, 1)
            if 3 <= s + 2 < MKV_SLABS:
                low(s + 2)
            if s in (1, 2):
                mem_low(1, range((s - 1) * KT // 2, s * KT // 2))
            for m in X_BESIDE[s - 1] if s else ():
                x_low(0, m, 0)
        for m in X_BESIDE[MKV_SLABS - 1]:
            x_low(0, m, 0)

        def tile_out(slab, tpar, outs):
            dve.wait_ge(slab_done, slab + 1)
            for out, rows, scale in outs:
                src = acc[rows, tpar, :, 0:HALF]
                if scale is None:
                    last = dve.tensor_tensor(halves(out), src, halves(rstd[rows, :]), ALU.mult)
                else:
                    last = dve.scalar_tensor_tensor(out=halves(out), in0=src, scalar=scale,
                                                    in1=halves(rstd[rows, :]), op0=ALU.mult, op1=ALU.mult)
            return last

        def queries(slab, tpar, par, scale):
            dve.wait_ge(slab_done, slab + 1)
            for hd in range(2):
                rows, cols = slice(hd * HD, (hd + 1) * HD), slice(hd * DEC, (hd + 1) * DEC)
                dve.scalar_tensor_tensor(out=qs[par][rows, cols], in0=acc[rows, tpar, 0, 0:DEC], scalar=scale,
                                         in1=rstd[rows, 0:DEC], op0=ALU.mult, op1=ALU.mult)
            return tile_out(slab, tpar, [(qz[par][0:HD, 0, :], slice(0, HD), scale),
                                         (qz[par][HD:P, 1, :], slice(HD, P), scale)])

        def front(c, u):
            b, w, sample = c.buf(u), c.width(u), u == 2 * QT
            hd, i = divmod(u, QT)
            wide = work_a[:, b, 0:w]
            if c.stick:
                dve.wait_ge(probs_ready, c.unit + (u - 1))
                dve.wait_ge(soft_ready, c.pair * UNITS + (u + 1))
                tail = work_c[:, b, 0:w]
                for z, cols in c.parts(u):
                    dve.scalar_tensor_tensor(out=work_a[:, b, cols], in0=z, scalar=0.0, in1=work_c[:, b, cols],
                                             op0=ALU.max, op1=ALU.add)
                dve.drain()
                dve.tensor_tensor_scan(tail[:, ::-1], wide[:, ::-1], wide[:, ::-1], 0.0,
                                       ALU.add, ALU.bypass)
                dve.drain()
                for z, cols in c.parts(u):
                    last = dve.tensor_tensor(work_a[:, b, cols], z, work_c[:, b, cols], ALU.subtract)
                last.then_inc(exp_in, 1)
                dve.drain()
                dve.sem_inc(score_free, 1)
                return
            dve.wait_ge(score_ready, c.used(u))
            if c.mem:
                dve.tensor_copy(wide, score[:, b, 0:w])
            else:
                if u == 0:
                    dve.wait_ge(cum_in[c.par], c.cums)
                if sample:
                    gate_q, gate_k = cq_s[:, bass.ds(c.pair, 1)], ckbs[c.par]
                else:
                    gate_q, gate_k = cq[:, i, bass.ds(c.pair * 2 + hd, 1)], ckb[c.par][:, hd, :]
                for z, cols in c.parts(u):
                    dve.scalar_tensor_tensor(out=work_a[:, b, cols], in0=z, scalar=gate_q,
                                             in1=gate_k[:, cols], op0=ALU.subtract, op1=ALU.add)
                dve.drain()
                const, n = (C_FOXS, DEC) if sample else (C_FOX, P)
                diag = work_a[:, b, w - n:w]
                dve.tensor_tensor(diag, diag, cst[:, const:const + n], ALU.add)
            dve.drain()
            dve.sem_inc(score_free, 1)
            dve.tensor_reduce(least[:, b:b + 1], wide, AX, ALU.min).then_inc(exp_in, 1)

        def normalize(c, u):
            b, w = c.buf(u), c.width(u)
            dve.wait_ge(exp_out, c.unit + (u + 1))
            dve.reciprocal(inv[:, b:b + 1], total[:, b:b + 1])
            dve.drain()
            dve.tensor_scalar(work_b[:, b, 0:w], work_b[:, b, 0:w], inv[:, b:b + 1], None,
                              ALU.mult).then_inc(probs_ready, 1)

        def out_low(c, n):
            dve.wait_ge(out_hi, c.out + (n + 1))
            tile = bass.ds(c.o_tile, 1)
            for hd in range(2):
                if n != 1 - hd:
                    rows = slice(hd * HD, (hd + 1) * HD)
                    cols = slice(0, DEC) if n == 2 else slice(DEC, TOK)
                    src = c.sample_out()[rows, hd * DEC:(hd + 1) * DEC] if n == 2 else out_ps[rows, :]
                    last = dve.tensor_tensor(o_lo[rows, tile, cols],
                                             src.rearrange("p (a c) -> p a c", a=1),
                                             o_hi[rows, tile, cols].bitcast(F32), ALU.subtract)
            last.then_inc(out_free, 1)

        def fill_out(c, n):
            (t, what), slab = c.tiles[n], c.slabs[n]
            par = 0 if c.mem else 1 - c.par
            if what == "q":
                last = queries(slab, t % 2, par, -SCALE if c.layer == 0 else SCALE)
            elif what == "k":
                last = tile_out(slab, t % 2, [(kb[par][:, PAST:], slice(0, P), None)])
            else:
                if not c.mem:
                    dve.wait_ge(kv_stored, (c.a + (c.layer * PAIRS - 1)) * 32)
                else:
                    at_least(dve, kv_stored, c.layer * PAIRS * 32)
                last = tile_out(slab, t % 2, [(vf[:, :], slice(0, P), None)])
            last.then_inc(qkv_ready, 1)
            dve.drain()
            dve.sem_inc(acc_free, 1)

        def attention(c, prev, nxt):
            if prev is None:
                front(c, 0)
            for u in range(UNITS):
                early = u + 1 == UNITS and nxt is not None and nxt.stick and not c.stick
                if early:
                    normalize(c, u)
                if u + 1 < UNITS:
                    front(c, u + 1)
                elif nxt is not None:
                    front(nxt, 0)
                if not c.stick and not early:
                    normalize(c, u)
                if u < 2 and prev is not None:
                    out_low(prev, u + 1)
                if u == QT + 1:
                    out_low(c, 0)
                if u in c.ends and c.tiles[0][1] != "o":
                    fill_out(c, c.ends.index(u))
            if nxt is None:
                out_low(c, 1)
                out_low(c, 2)

        for layer in range(DEPTH):
            s0 = layer_slab(layer)
            dve.wait_ge(rstd_made, 2 * layer + 2)
            queries(s0, 0, 0, -SCALE).then_inc(qkv_ready, 1)
            dve.drain()
            dve.sem_inc(acc_free, 1)
            if layer == 0:
                y = work_a[0:HEADS, 0, :]
                dve.wait_ge(score_ready, LAYER_USE[layer] + 4)
                dve.tensor_tensor(halves(y), score[0:HEADS, :, 0:HALF], halves(rstd[0:HEADS, :]), ALU.mult)
                dve.drain()
                dve.sem_inc(score_free, 2)
                dve.wait_ge(wf_in, 32)
                dve.tensor_scalar(y, y, bias_f[:, 0:1], None, ALU.add).then_inc(gate_in, 1)
                dve.wait_ge(gate_soft, 1)
                dve.scalar_tensor_tensor(out=lf[:, PAST:], in0=y, scalar=0.0, in1=work_b[0:HEADS, 0, :],
                                         op0=ALU.min, op1=ALU.subtract)
                dve.drain()
                dve.wait_ge(clf_in, 16)
                for c0, c1 in ((0, KEYS_S), (KEYS_S, PAST + TOK)):
                    dve.tensor_tensor_scan(cum[:, c0:c1], lf[:, c0:c1], lf[:, c0:c1], 0.0,
                                           ALU.add, ALU.bypass)
                dve.drain()
                dve.tensor_copy(dup[:, 0:DEC], cum[:, PAST:KEYS_S])
                dve.tensor_copy(dup[:, DEC:P], cum[:, PAST:KEYS_S]).then_inc(cum_made, 1)
            queries(s0 + 1, 1, 1, -SCALE).then_inc(qkv_ready, 1)
            dve.drain()
            dve.sem_inc(acc_free, 1)
            if layer == 0:
                dve.wait_ge(turned_free, 2 * DEPTH + 1)
            calls(dve, layer, attention)

            def residual(slab, m):
                dve.wait_ge(slab_done, slab + 1)
                dve.tensor_tensor(halves(x[:, m, :]), acc[:, m % 2, :, 0:HALF], halves(x[:, m, :]),
                                  ALU.add).then_inc(x_new, 1)
                dve.drain()
                dve.sem_inc(acc_free, 1)

            for m in range(OUT_TILES):
                residual(s0 + IN_TILES + m, m)
                if m == 0:
                    low(s0 + IN_TILES + 2)
                x_low(2 * layer + 1, m, 4 + layer)
            sg = gu_slab(layer)
            dve.wait_ge(rstd_made, 2 * layer + 3)

            def gate_up(j):
                n = layer * FT + 1
                tile_out(j * 2 + sg, 0, [(work_a[:, 0, :], slice(0, P), None)]).then_inc(gated, 1)
                dve.drain()
                dve.sem_inc(acc_free, 1)
                tile_out(j * 2 + (sg + 1), 1, [(work_c[:, 0, :], slice(0, P), None)])
                dve.drain()
                dve.sem_inc(acc_free, 1)
                dve.wait_ge(silu_made, j + n)
                dve.tensor_tensor(work_c[:, 0, :], work_c[:, 0, :], work_b[:, 0, :], ALU.mult) \
                    .then_inc(prod_made, 1)
                dve.wait_ge(fhi_made, j + n)
                dve.tensor_tensor(f_lo[:, bass.ds(j, 1), :], work_c[:, 0:1, :],
                                  f_hi[:, bass.ds(j, 1), :].bitcast(F32), ALU.subtract).then_inc(flo_made, 1)

            with dve.Fori(0, FT) as j:
                gate_up(j)
            sd = sg + GU_TILES
            for m in range(KT):
                residual(sd + 3 * m + 2, m)
                if layer < DEPTH - 1:
                    x_low(2 * layer + 2, m, 1)
        dve.wait_ge(rstd_made, 2 * DEPTH + 2)
        for k in (k for k in range(KT) if k not in POOL_OUT):
            dve.scalar_tensor_tensor(out=x[:, k, :], in0=x[:, k, :],
                                     scalar=gain[:, 6 * KT + k:6 * KT + k + 1], in1=rstd[:, :],
                                     op0=ALU.mult, op1=ALU.mult).then_inc(y_made, 1)

    ctx.close()


def _tiles(w, kt=KT):
    rows, cols = w.shape
    return np.ascontiguousarray(
        w.reshape(kt, P, cols // P, P).transpose(2, 1, 0, 3).reshape(cols // P, P, kt * P))


def _feature_major(a):
    return np.ascontiguousarray(a.T.reshape(-1, P, a.shape[0]).transpose(1, 0, 2))


def _consts():
    q, k = np.arange(P)[:, None], np.arange(P)[None, :]
    qs, ks = np.arange(P)[:, None] % DEC, np.arange(DEC)[None, :]
    out = np.zeros((P, C_END), np.float32)
    out[:, C_ID:C_ID + P] = q == k
    out[:, C_MEAN:C_MEAN + P] = 1.0 / D_MODEL
    out[:, C_FOX:C_FOX + P] = np.where(k > q, BIG, 0.0)
    out[:, C_FOXS:C_FOXS + DEC] = np.where(ks > qs, BIG, 0.0)
    out[:, C_SBN:C_SBN + P] = np.where(k >= q, -BIG, 0.0)
    out[:, C_SBNS:C_SBNS + DEC] = np.where(ks >= qs, -BIG, 0.0)
    return out


def kernel(x_prompt, x_sample, mem_prompt, cache_fox_k, cache_fox_v, cache_fox_logf, cache_sb_k,
           cache_sb_v, cache_mem_k, cache_mem_v, g_mix, w_in_fox, b_f, w_in_sb, g_mem, w_mem_kv,
           w_out, g_ffn, w_gate_up, w_down, g_final):
    import concourse.bacc as bacc
    from concourse.bass_utils import run_bass_kernel_spmd

    A = np.asarray
    W = HEADS * HD
    order = [slice(3 * W, 3 * W + P), slice(3 * W + P, 3 * W + 2 * P)]
    for p in range(PAIRS):
        order += [slice(g * W + p * P, g * W + (p + 1) * P) for g in ((0, 1, 2) if p else (1, 0, 2))]
    fox, stick = A(w_in_fox)[0], A(w_in_sb)[0]
    gate_w = fox[:, 3 * W:3 * W + HEADS]
    fox = np.concatenate([fox[:, :3 * W], fox[:, 3 * W + HEADS:]], axis=1)
    w_in = np.stack([_tiles(np.concatenate([w[:, s] for s in order], axis=1)) for w in (fox, stick)])
    gu = A(w_gate_up)
    gu = gu.reshape(DEPTH, D_MODEL, 2, FT, P).transpose(0, 1, 3, 2, 4).reshape(DEPTH, D_MODEL, 2 * D_FF)
    gains = np.concatenate([A(g_mix), A(g_mem), A(g_ffn), A(g_final)[None]])

    def keys(c):
        return c.reshape(c.shape[0], -1, P).transpose(1, 2, 0)

    def vals(c):
        n = c.shape[0] // P
        return c.reshape(n, P, -1, P).transpose(2, 1, 0, 3).reshape(-1, P, n * P)

    arrays = {
        "x_t": _feature_major(np.concatenate([A(x_sample)[0], A(x_prompt)[0]])),
        "mem_t": _feature_major(A(mem_prompt)[0]),
        "w_mkv": np.stack([_tiles(w) for w in A(w_mem_kv)]),
        "w_in": w_in,
        "w_f": gate_w.reshape(KT, P, HEADS).transpose(1, 0, 2).reshape(P, KT * HEADS),
        "w_out": np.stack([_tiles(w) for w in A(w_out)]),
        "w_gu": np.stack([_tiles(w) for w in gu]),
        "w_dn": np.stack([_tiles(w, FT) for w in A(w_down)]),
        "gains": gains.reshape(7, KT, P).transpose(2, 0, 1).reshape(P, 7 * KT),
        "b_f": A(b_f)[0][:, None],
        "ck": np.stack([keys(A(cache_fox_k)[0, 0]), keys(A(cache_sb_k)[0, 0])]),
        "cv": np.stack([vals(A(cache_fox_v)[0, 0]), vals(A(cache_sb_v)[0, 0])]),
        "clf": A(cache_fox_logf)[0, 0].T,
        "cmk": np.stack([keys(c[0]) for c in A(cache_mem_k)]),
        "cmv": np.stack([vals(c[0]) for c in A(cache_mem_v)]),
        "consts": _consts(),
    }
    outs = {
        "y_t": (P, KT, TOK),
        "k_o": (DEPTH, PAIRS, P, TOK),
        "v_o": (DEPTH, PAIRS, P, TOK),
        "lf_o": (HEADS, TOK),
        "mk_o": (DEPTH, MEM_PAIRS, P, N_MEM),
        "mv_o": (DEPTH, MEM_PAIRS, P, N_MEM),
    }
    nc = bacc.Bacc("TRN2", target_bir_lowering=False, num_devices=1)
    arrays = {n: np.ascontiguousarray(a) for n, a in arrays.items()}
    args = {n: nc.dram_tensor("in_" + n, a.shape, F32, kind="ExternalInput").ap() for n, a in arrays.items()}
    args |= {n: nc.dram_tensor("out_" + n, s, F32, kind="ExternalOutput").ap() for n, s in outs.items()}
    build(nc, **args)
    r = run_bass_kernel_spmd(nc, [{"in_" + n: a for n, a in arrays.items()}], core_ids=[0])
    got = {n: r.results[0]["out_" + n] for n in outs}

    y = got["y_t"].transpose(2, 1, 0).reshape(TOK, D_MODEL)

    def heads(a, part):
        return a[:, :, part].transpose(2, 0, 1).reshape(1, 1, -1, HEADS, HD)

    def mem(a):
        return a.transpose(0, 3, 1, 2).reshape(DEPTH, 1, N_MEM, MEM_HEADS, HD)

    sample, prompt = slice(0, DEC), slice(DEC, TOK)
    out = {}
    for name, part in (("p", prompt), ("s", sample)):
        out[name] = (heads(got["k_o"][0], part), heads(got["v_o"][0], part),
                     got["lf_o"][:, part].T[None, None],
                     heads(got["k_o"][1], part), heads(got["v_o"][1], part))
    result = (y[prompt][None], y[sample][None], *out["p"], mem(got["mk_o"]), mem(got["mv_o"]), *out["s"])
    return tuple(np.ascontiguousarray(a) for a in result)
```
